# Optimizing a Trainium2 kernel written in Bass

```python
import math
import jax, jax.numpy as jnp
from jax import lax
import numpy as np

D_MODEL = 1024
BATCH = 1
SEQ = 256
DEPTH = 4

N_MIXERS = 3
FOX_HEADS = 16
FOX_HEAD_DIM = D_MODEL // FOX_HEADS
Q_BLOCK = 128
S5_GROUP = 16
S5_GROUPS = D_MODEL // S5_GROUP
S5_STATE = 64
SCAN_CHUNK = 128
POOL_WINDOWS = (2, 4, 8, 16)
POOL_GROUP = D_MODEL // len(POOL_WINDOWS)
D_FF = ((8 * D_MODEL + 3 * 256 - 1) // (3 * 256)) * 256
DN_ALPHA = (2.0 * DEPTH) ** 0.25
DN_BETA = (8.0 * DEPTH) ** -0.25
LN_EPS = 1e-5
N_FOX = (DEPTH + 2) // 3
N_S5 = (DEPTH + 1) // 3
N_POOL = DEPTH // 3

kernel_name = "fox_s5_pool_interleaved_deepnorm"

def layer_norm(h, g, b):
    h32 = h.astype(jnp.float32)
    mu = jnp.mean(h32, axis=-1, keepdims=True)
    var = jnp.mean(jnp.square(h32 - mu), axis=-1, keepdims=True)
    return ((h32 - mu) * lax.rsqrt(var + LN_EPS) * g + b).astype(h.dtype)

def fox_mixer(x, w_qkv, w_f, b_f, w_o):
    bsz, s, _ = x.shape
    q, k, v = jnp.split(x @ w_qkv, 3, axis=-1)
    q = q.reshape(bsz, s, FOX_HEADS, FOX_HEAD_DIM)
    k = k.reshape(bsz, s, FOX_HEADS, FOX_HEAD_DIM)
    v = v.reshape(bsz, s, FOX_HEADS, FOX_HEAD_DIM)
    log_f = jax.nn.log_sigmoid((x @ w_f + b_f).astype(jnp.float32))
    c = jnp.cumsum(log_f, axis=1)
    c_k = jnp.transpose(c, (0, 2, 1))
    nb = s // Q_BLOCK
    q_blocks = q.reshape(bsz, nb, Q_BLOCK, FOX_HEADS, FOX_HEAD_DIM).transpose(1, 0, 2, 3, 4)
    c_blocks = c.reshape(bsz, nb, Q_BLOCK, FOX_HEADS).transpose(1, 0, 3, 2)
    k_pos = jnp.arange(s)
    scale = FOX_HEAD_DIM ** -0.5

    def block(args):
        qb, cb, i = args
        logits = jnp.einsum('bqhd,bkhd->bhqk', qb, k).astype(jnp.float32) * scale
        logits = logits + cb[..., :, None] - c_k[..., None, :]
        q_pos = i * Q_BLOCK + jnp.arange(Q_BLOCK)
        mask = k_pos[None, :] <= q_pos[:, None]
        logits = jnp.where(mask, logits, -jnp.inf)
        p = jax.nn.softmax(logits, axis=-1).astype(v.dtype)
        return jnp.einsum('bhqk,bkhd->bqhd', p, v)

    o = lax.map(block, (q_blocks, c_blocks, jnp.arange(nb)))
    o = o.transpose(1, 0, 2, 3, 4).reshape(bsz, s, D_MODEL)
    return o @ w_o

def s5_mixer(x, w_in, a_re, a_im, log_dt, b_re, b_im, c_re, c_im, d_skip, w_glu, b_glu):
    bsz, s, _ = x.shape
    f32 = jnp.float32
    u = x @ w_in
    u32 = u.astype(f32).reshape(bsz, s, S5_GROUPS, S5_GROUP)
    dt = jnp.exp(log_dt.astype(f32))[:, None]
    ar, ai = a_re.astype(f32), a_im.astype(f32)
    mag = jnp.exp(ar * dt)
    lr, li = mag * jnp.cos(ai * dt), mag * jnp.sin(ai * dt)
    den = ar * ar + ai * ai
    zr = ((lr - 1.0) * ar + li * ai) / den
    zi = (li * ar - (lr - 1.0) * ai) / den
    br, bi = b_re.astype(f32), b_im.astype(f32)
    bbr = zr[..., None] * br - zi[..., None] * bi
    bbi = zr[..., None] * bi + zi[..., None] * br
    cr, ci = c_re.astype(f32), c_im.astype(f32)
    nc = s // SCAN_CHUNK
    u_chunks = u32.reshape(bsz, nc, SCAN_CHUNK, S5_GROUPS, S5_GROUP).transpose(1, 0, 2, 3, 4)

    def combine(e1, e2):
        a1r, a1i, b1r, b1i = e1
        a2r, a2i, b2r, b2i = e2
        return (a2r * a1r - a2i * a1i,
                a2r * a1i + a2i * a1r,
                a2r * b1r - a2i * b1i + b2r,
                a2r * b1i + a2i * b1r + b2i)

    def chunk_step(carry, uc):
        h0r, h0i = carry
        bur = jnp.einsum('gpc,blgc->blgp', bbr, uc)
        bui = jnp.einsum('gpc,blgc->blgp', bbi, uc)
        lam_r = jnp.broadcast_to(lr, bur.shape)
        lam_i = jnp.broadcast_to(li, bur.shape)
        pr, pi, hr, hi = lax.associative_scan(combine, (lam_r, lam_i, bur, bui), axis=1)
        hr, hi = (hr + pr * h0r[:, None] - pi * h0i[:, None],
                  hi + pr * h0i[:, None] + pi * h0r[:, None])
        y = jnp.einsum('gcp,blgp->blgc', cr, hr) - jnp.einsum('gcp,blgp->blgc', ci, hi)
        return (hr[:, -1], hi[:, -1]), y

    init = (jnp.zeros((bsz, S5_GROUPS, S5_STATE), f32),
            jnp.zeros((bsz, S5_GROUPS, S5_STATE), f32))
    _, y = lax.scan(chunk_step, init, u_chunks)
    y = y.transpose(1, 0, 2, 3, 4).reshape(bsz, s, D_MODEL)
    y = y + d_skip.astype(f32) * u32.reshape(bsz, s, D_MODEL)
    y = jax.nn.gelu(y).astype(x.dtype)
    val, gate = jnp.split(y @ w_glu + b_glu, 2, axis=-1)
    return val * jax.nn.sigmoid(gate)

def pool_mixer(x, w_in, w_grp, scale, w_out):
    bsz, s, _ = x.shape
    u32 = (x @ w_in).astype(jnp.float32)
    cs = jnp.cumsum(u32, axis=1)
    pos1 = jnp.arange(1, s + 1)
    outs = []
    for gi, w in enumerate(POOL_WINDOWS):
        sl = slice(gi * POOL_GROUP, (gi + 1) * POOL_GROUP)
        csg = cs[..., sl]
        lag = jnp.pad(csg, ((0, 0), (w, 0), (0, 0)))[:, :s]
        cnt = jnp.minimum(pos1, w).astype(jnp.float32)[None, :, None]
        outs.append((csg - lag) / cnt - u32[..., sl])
    m = jnp.stack(outs, axis=2).astype(x.dtype)
    m = jnp.einsum('bsgc,gcd->bsgd', m, w_grp).reshape(bsz, s, D_MODEL)
    return (m * scale) @ w_out

def swiglu(x, w1, w3, w2):
    return (jax.nn.silu(x @ w1) * (x @ w3)) @ w2

def setup_inputs(seed: int = 0) -> dict:
    key = jax.random.key(seed)
    ks = jax.random.split(key, 32)
    f32 = jnp.float32

    def nrm(k, shape, sc):
        return jax.random.normal(k, shape, f32) * sc

    d = D_MODEL
    a_im_base = math.pi * jnp.arange(S5_STATE, dtype=f32)
    return {
        "x": nrm(ks[0], (BATCH, SEQ, d), 1.0),
        "ln_g": 1.0 + nrm(ks[1], (DEPTH, 2, d), 0.02),
        "ln_b": nrm(ks[2], (DEPTH, 2, d), 0.02),
        "fox_w_qkv": nrm(ks[3], (N_FOX, d, 3 * d), d ** -0.5),
        "fox_w_f": nrm(ks[4], (N_FOX, d, FOX_HEADS), 0.1 * d ** -0.5),
        "fox_b_f": jax.random.uniform(ks[5], (N_FOX, FOX_HEADS), f32, 1.0, 6.0),
        "fox_w_o": nrm(ks[6], (N_FOX, d, d), DN_BETA * d ** -0.5),
        "s5_w_in": nrm(ks[7], (N_S5, d, d), d ** -0.5),
        "s5_a_re": -0.5 + nrm(ks[8], (N_S5, S5_GROUPS, S5_STATE), 0.01),
        "s5_a_im": a_im_base + nrm(ks[9], (N_S5, S5_GROUPS, S5_STATE), 0.01),
        "s5_log_dt": jax.random.uniform(ks[10], (N_S5, S5_GROUPS), f32, math.log(1e-3), math.log(1e-1)),
        "s5_b_re": nrm(ks[11], (N_S5, S5_GROUPS, S5_STATE, S5_GROUP), (2 * S5_GROUP) ** -0.5),
        "s5_b_im": nrm(ks[12], (N_S5, S5_GROUPS, S5_STATE, S5_GROUP), (2 * S5_GROUP) ** -0.5),
        "s5_c_re": nrm(ks[13], (N_S5, S5_GROUPS, S5_GROUP, S5_STATE), S5_STATE ** -0.5),
        "s5_c_im": nrm(ks[14], (N_S5, S5_GROUPS, S5_GROUP, S5_STATE), S5_STATE ** -0.5),
        "s5_d": nrm(ks[15], (N_S5, d), 1.0),
        "s5_w_glu": nrm(ks[16], (N_S5, d, 2 * d), DN_BETA * d ** -0.5),
        "s5_b_glu": nrm(ks[17], (N_S5, 2 * d), 0.02),
        "pool_w_in": nrm(ks[18], (N_POOL, d, d), d ** -0.5),
        "pool_w_grp": nrm(ks[19], (N_POOL, len(POOL_WINDOWS), POOL_GROUP, POOL_GROUP), POOL_GROUP ** -0.5),
        "pool_scale": 1.0 + nrm(ks[20], (N_POOL, d), 0.02),
        "pool_w_out": nrm(ks[21], (N_POOL, d, d), DN_BETA * d ** -0.5),
        "ffn_w1": nrm(ks[22], (DEPTH, d, D_FF), d ** -0.5),
        "ffn_w3": nrm(ks[23], (DEPTH, d, D_FF), d ** -0.5),
        "ffn_w2": nrm(ks[24], (DEPTH, D_FF, d), DN_BETA * D_FF ** -0.5),
    }

def reference(x, ln_g, ln_b,
              fox_w_qkv, fox_w_f, fox_b_f, fox_w_o,
              s5_w_in, s5_a_re, s5_a_im, s5_log_dt, s5_b_re, s5_b_im, s5_c_re, s5_c_im,
              s5_d, s5_w_glu, s5_b_glu,
              pool_w_in, pool_w_grp, pool_scale, pool_w_out,
              ffn_w1, ffn_w3, ffn_w2):
    h = x
    for i in range(DEPTH):
        kind, j = i % N_MIXERS, i // N_MIXERS
        if kind == 0:
            m = fox_mixer(h, fox_w_qkv[j], fox_w_f[j], fox_b_f[j], fox_w_o[j])
        elif kind == 1:
            m = s5_mixer(h, s5_w_in[j], s5_a_re[j], s5_a_im[j], s5_log_dt[j],
                         s5_b_re[j], s5_b_im[j], s5_c_re[j], s5_c_im[j],
                         s5_d[j], s5_w_glu[j], s5_b_glu[j])
        else:
            m = pool_mixer(h, pool_w_in[j], pool_w_grp[j], pool_scale[j], pool_w_out[j])
        h = layer_norm(DN_ALPHA * h + m, ln_g[i, 0], ln_b[i, 0])
        h = layer_norm(DN_ALPHA * h + swiglu(h, ffn_w1[i], ffn_w3[i], ffn_w2[i]), ln_g[i, 1], ln_b[i, 1])
    return h


_drawn_inputs = setup_inputs


def setup_inputs(seed=0):
    import zlib

    import numpy as np

    out = dict(_drawn_inputs(seed))
    spreads = {}
    factors = {'fox_w_f': 37.087,
     's5_a_re': 64.0,
     's5_a_im': 64.0,
     's5_log_dt': 64.0,
     's5_b_re': 64.0,
     's5_b_im': 64.0,
     's5_c_re': 64.0,
     's5_c_im': 64.0,
     's5_b_glu': 28.294,
     'pool_scale': 76.324}
    for name, (base, spread) in spreads.items():
        noise = np.random.default_rng([zlib.crc32(name.encode()), seed]).standard_normal(out[name].shape)
        drawn = base * np.exp(spread * noise) if base else spread * noise
        out[name] = __import__('jax').numpy.asarray(drawn.astype(out[name].dtype))
    for name, factor in factors.items():
        out[name] = (out[name] * factor).astype(out[name].dtype)
    return out
```

```python
from contextlib import ExitStack

import numpy as np

import concourse.bass as bass
from concourse import mybir

F32 = mybir.dt.float32
F32R = mybir.dt.float32r
I32 = mybir.dt.int32
ALU = mybir.AluOpType
ACT = mybir.ActivationFunctionType
AX_X = mybir.AxisListType.X

P = 128
SEQ = 256
D = 1024
KC = D // P
TM = SEQ // P
HALF = 512
DEPTH = 4
D_FF = 2816
FCH = D_FF // P
HEADS, HD = 16, 64
PAIRS = HEADS // 2
GROUPS, GC, ST = 64, 16, 64
STEP = P // GC
NBLK = SEQ // STEP
WINDOWS = (2, 4, 8, 16)
ALPHA = (2.0 * DEPTH) ** 0.25
LN_EPS = 1e-5
NEG = -1.0e30

RAW = 6
SPL = 3

T_FOX = KC + 2 * PAIRS + KC
T_S5 = KC + 2 * KC
T_POOL = KC + 2 + KC
T_FFN = 3 * FCH
MIXERS = ("fox", "s5", "pool", "fox")
MIX_TILES = {"fox": T_FOX, "s5": T_S5, "pool": T_POOL}

C_ID = 0
C_PERM = C_ID + P
C_MASK = C_PERM + P
C_HOT = C_MASK + 2 * P
C_SGN = C_HOT + HEADS
C_NSGN = C_SGN + 1
C_EPS = C_NSGN + 1
C_ID16 = C_EPS + 1
C_INV = C_ID16 + GC
C_N = C_INV + 4 * 16

EXP_C = [1 / 5040, 1 / 720, 1 / 120, 1 / 24, 1 / 6, 0.5]
LN2_HI, LN2_LO = 0.693145751953125, 1.42860677e-06
TWO_PI = (6.28125, 0.0019350051879882812, 3.019916e-07)
MAGIC = 12582912.0


def constants():
    c = np.zeros((P, C_N), np.float32)
    i = np.arange(P)
    c[:, C_ID:C_ID + P] = np.eye(P)
    c[i, C_PERM + (i + ST) % P] = 1.0
    tri = np.where(i[None, :] <= i[:, None], 0.0, NEG)
    c[:, C_MASK + P:C_MASK + 2 * P] = tri
    c[HD:HD + HEADS, C_HOT:C_HOT + HEADS] = np.eye(HEADS)
    c[:, C_SGN] = np.where(i < ST, -1.0, 1.0)
    c[:, C_NSGN] = -c[:, C_SGN]
    c[:, C_EPS] = LN_EPS
    c[i, C_ID16 + i % GC] = 1.0
    for w, win in enumerate(WINDOWS):
        c[:, C_INV + 16 * w:C_INV + 16 * w + 16] = 1.0 / np.minimum(np.arange(1, 17), win)
    return c


def build(nc, t, layers=DEPTH, last_ffn=True):
    starts = []
    at = 0
    for l in range(layers):
        starts.append(at)
        at += MIX_TILES[MIXERS[l]] + T_FFN
    n_tiles = at
    n_ln = 2 * layers

    with ExitStack() as ctx:
        def sb(name, shape, dt=F32):
            return ctx.enter_context(nc.sbuf_tensor(name, shape, dt))

        def sem(name):
            return ctx.enter_context(nc.semaphore(name))

        bank = [ctx.enter_context(nc.psum_tensor(f"bank{i}", [P, HALF], F32)) for i in range(8)]

        cst = sb("cst", [P, C_N])
        raw = sb("raw", [P, RAW, D])
        whi = sb("whi", [P, SPL, D], F32R)
        wlo = sb("wlo", [P, SPL, D], F32R)
        x_tm = sb("x_tm", [P, TM, D])
        xhi = sb("xhi", [P, KC, SEQ], F32R)
        xlo = sb("xlo", [P, KC, SEQ], F32R)
        silu = sb("silu", [P, SEQ])
        hval = sb("hval", [P, SEQ])
        hhi = sb("hhi", [P, 2, SEQ], F32R)
        hlo = sb("hlo", [P, 2, SEQ], F32R)
        ln_col = sb("ln_col", [P, 2, 2 * DEPTH, KC])
        stats = sb("stats", [P, TM, 2, 6])
        mv = sb("mv", [P, TM, 2])
        std = sb("std", [P, TM, 1])
        rstd = sb("rstd", [P, TM, 1])
        slot = [sb(f"slot{i}", [P, 2 * D]) for i in range(5)]
        smx = sb("smx", [P, 2, 8])
        wf = sb("wf", [P, 2, KC, HEADS])
        bf = sb("bf", [HEADS, 2])
        prm = sb("prm", [P, 3, GROUPS])
        dcol = sb("dcol", [P, 16])
        lam = sb("lam", [P, 2, STEP, GROUPS])
        pscale = sb("pscale", [P, KC])
        mag8 = sb("mag8", [P, GROUPS])

        def overlay(*specs):
            with ExitStack() as inner:
                return [inner.enter_context(nc.sbuf_tensor(n, s, d)) for n, s, d in specs]

        KQ = HD + HEADS
        ohi, olo = overlay(("ohi", [P, KC, SEQ], F32R), ("olo", [P, KC, SEQ], F32R))
        cosT, sinT = overlay(("cosT", [P, GROUPS, NBLK], F32), ("sinT", [P, GROUPS, NBLK], F32))
        sb("held", [P, 2 * KC * SEQ])
        qa, ka, vt, sc, pT, zg, ones = overlay(
            ("qa", [KQ, HEADS, SEQ], F32), ("ka", [KQ, HEADS, SEQ], F32), ("vt", [P, TM, D], F32),
            ("sc", [P, 2, 3 * P], F32), ("pT", [P, 2, 3 * P], F32), ("zg", [HEADS, 4, SEQ], F32), ("ones", [HEADS, SEQ], F32))
        BT = sb("BT", [P, GROUPS, P])
        CT = sb("CT", [P, GROUPS, STEP, GC])
        ones_row = CT[0:1, 0, :, :].rearrange("p d c -> p (d c)")
        bglu = BT[0:1, 0:16, :].rearrange("p g n -> p (g n)")

        res = slot[0][:, :].rearrange("p (m d) -> p m d", m=TM)
        xval = slot[4][:, :].rearrange("p (b c) -> p b c", b=4)
        gb = slot[2][:, :].rearrange("p (k d) -> p k d", k=2)

        raw_landed = [sem(f"raw_landed{i}") for i in range(RAW)]
        w_hi, w_lo, w_used = sem("w_hi"), sem("w_lo"), sem("w_used")
        small_landed = sem("small_landed")
        later_landed, x_landed, bglu_landed = sem("later_landed"), sem("x_landed"), sem("bglu_landed")
        sub_done = sem("sub_done")
        var_ready, std_ready, xn_ready = sem("var_ready"), sem("std_ready"), sem("xn_ready")
        xnT_ready, xval_ready, xhi_ready, xT_ready = sem("xnT_ready"), sem("xval_ready"), sem("xhi_ready"), sem("xT_ready")
        gb_landed, x_ready = sem("gb_landed"), sem("x_ready")
        silu_ready = sem("silu_ready")
        h_ready, hhi_ready, hlo_ready = sem("h_ready"), sem("hhi_ready"), sem("hlo_ready")
        dve_own, act_own, pool_own = sem("dve_own"), sem("act_own"), sem("pool_own")
        stored = sem("stored")
        gate_ps, gate_z, gate_l, ka_rows, qa_rows = sem("gate_ps"), sem("gate_z"), sem("gate_l"), sem("ka_rows"), sem("qa_rows")
        v_sb, q_sb, k_sb = sem("v_sb"), sem("q_sb"), sem("k_sb")
        s_ps, s_sb, e_sb, p_sb = sem("s_ps"), sem("s_sb"), sem("e_sb"), sem("p_sb")
        pT_ps, pT_sb, o_ps, ohi_sb, olo_sb = sem("pT_ps"), sem("pT_sb"), sem("o_ps"), sem("ohi_sb"), sem("olo_sb")
        prm_act, prm_dve = sem("prm_act"), sem("prm_dve")
        lam_ready, ct_ready, wb_ready = sem("lam_ready"), sem("ct_ready"), sem("wb_ready")
        wb_ps, bt_sb, bt_sb2, m_ps, m_sb, m_sb2, m_d, m_st, zero_st, tables = (
            sem(n) for n in ("wb_ps", "bt_sb", "bt_sb2", "m_ps", "m_sb", "m_sb2", "m_d", "m_st", "zero_st", "tables"))
        ug_sb = sem("ug_sb")
        tp_ld = [sem(f"tp_ld{j}") for j in range(4)]
        u_sb, u2_ld, uT_ps, uT_sb = sem("u_sb"), sem("u2_ld"), sem("uT_ps"), sem("uT_sb")
        st_ps, st_sb, sw_ps, rot_sb, g_sb, gw_ps, hs_sb = (sem(n) for n in ("st_ps", "st_sb", "sw_ps", "rot_sb", "g_sb", "gw_ps", "hs_sb"))
        y_ps, y_sb, yt_ld, yT_ps, yhi_sb, ylo_sb = (sem(n) for n in ("y_ps", "y_sb", "yt_ld", "yT_ps", "yhi_sb", "ylo_sb"))
        glu_ps, sig_sb, glu_sb = sem("glu_ps"), sem("sig_sb"), sem("glu_sb")
        pads_zero = sem("pads_zero")
        pu_sb, pm_sb, phi_sb, plo_sb = sem("pu_sb"), sem("pm_sb"), sem("phi_sb"), sem("plo_sb")
        pg_ps, zhi_sb, zlo_sb = sem("pg_ps"), sem("zhi_sb"), sem("zlo_sb")

        ident = cst[:, C_ID:C_ID + P]
        sgn = cst[:, C_SGN:C_SGN + 1]
        nsgn = cst[:, C_NSGN:C_NSGN + 1]

        def g3(s, a=0, n=GROUPS, w=NBLK):
            return slot[s][:, a:a + n * w].rearrange("p (g n) -> p g n", g=n)
        u_tm = slot[0][:, :].rearrange("p (m d) -> p m d", m=TM)
        U2 = slot[1][:, :].rearrange("p (s c) -> p s c", s=STEP)
        Msb = slot[2][:, :].rearrange("p (g n) -> p g n", g=16)
        U2s = slot[1][:, :].rearrange("p (s g c) -> p g s c", s=STEP, g=16)
        Ug = slot[0][:, :].rearrange("p (g s c) -> p g s c", g=16, s=STEP)
        Ust, Ssb, rot = g3(2), g3(3), g3(4)
        BA, BB = (slot[1][:, i * D:(i + 1) * D].rearrange("p (g c) -> p g c", g=GROUPS) for i in range(2))
        CA, CB = (slot[3][:, i * D:(i + 1) * D].rearrange("p (g c) -> p g c", g=GROUPS) for i in range(2))
        y_tm = rot_tm = slot[4][:, :].rearrange("p (m d) -> p m d", m=TM)

        PADT = 16
        ub = [slot[1][:, i * 272:(i + 1) * 272] for i in range(6)]

        FIRST = [(cst[:, :], t["consts"]), (ln_col[:, :, :, :], t["ln_col"]), (wf[:, :, :, :], t["wf"]), (bf[:, :], t["bf"]),
                 (prm[:, :, :], t["s5_prm"])]
        LATER = [(dcol[:, :], t["s5_dcol"]), (slot[1][:, :], t["s5_B"]), (slot[3][:, :], t["s5_C"]),
                 (pscale[:, :], t["pool_scale"])]

        ctx.enter_context(nc.allow_low_precision(reason="float32r halves of float32 values")) if hasattr(nc, "allow_low_precision") else None
        block = ctx.enter_context(nc.Block())

        @block.sync
        def _(sp):
            sp.dma_start(x_tm[:, :, :], t["x"].rearrange("(m p) d -> p m d", m=TM)).then_inc(x_landed, 16)
            for dst, src in FIRST:
                sp.dma_start(dst, src).then_inc(small_landed, 16)
            for c in range(RAW):
                sp.dma_start(raw[:, c, :], t["w"][c]).then_inc(raw_landed[c], 16)
            for dst, src in LATER:
                sp.dma_start(dst, src).then_inc(later_landed, 16)
            rounds = n_tiles // RAW
            with sp.Fori(1, rounds) as i:
                for c in range(RAW):
                    sp.wait_ge(w_lo, RAW * i + (c + 1 - RAW))
                    sp.dma_start(raw[:, c, :], t["w"][RAW * i + c]).then_inc(raw_landed[c], 16)
            for c in range(n_tiles - rounds * RAW):
                sp.wait_ge(w_lo, RAW * (rounds - 1) + c + 1)
                sp.dma_start(raw[:, c, :], t["w"][RAW * rounds + c]).then_inc(raw_landed[c], 16)

        @block.gpsimd
        def _(pool):
            pool.wait_ge(small_landed, 16 * len(FIRST))
            if layers > 1:
                nc.gpsimd.memset(slot[2][:, 0:D], 0.0).then_inc(pool_own, 1)
                pool.wait_ge(pool_own, 1)
                for k in range(8):
                    pool.dma_start(t["toep"][:, k * D:(k + 1) * D], slot[2][:, 0:D]).then_inc(zero_st, 16)
                pool.wait_ge(zero_st, 16 * 8)
            own = [1 if layers > 1 else 0]

            def step(ins):
                own[0] += 1
                ins.then_inc(pool_own, 1)
                pool.wait_ge(pool_own, own[0])

            TT = nc.gpsimd.tensor_tensor
            TS = nc.gpsimd.tensor_scalar

            def cmul(yr, yi, ar, ai, br, bi, t1, t2):
                step(TT(t1, ar, br, ALU.mult))
                step(TT(t2, ai, bi, ALU.mult))
                step(TT(yr, t1, t2, ALU.subtract))
                step(TT(t1, ar, bi, ALU.mult))
                step(TT(t2, ai, br, ALU.mult))
                step(TT(yi, t1, t2, ALU.add))

            def s5_parameters():
                G = GROUPS

                def r(i, n=1):
                    return slot[0][:, i * G:(i + n) * G]
                pool.wait_ge(later_landed, 16 * len(LATER))
                pool.wait_ge(prm_act, 1)
                sn, cs, mag, den = r(6), r(7), r(8), r(2)
                ar, ai = prm[:, 0, :], prm[:, 1, :]
                pr, pi = lam[:, 0, :, :], lam[:, 1, :, :]
                step(TT(pr[:, 0, :], mag, cs, ALU.mult))
                step(TT(pi[:, 0, :], mag, sn, ALU.mult))
                ta = slot[0][:, 12 * G:16 * G].rearrange("p (d g) -> p d g", d=4)
                tb = slot[0][:, 16 * G:20 * G].rearrange("p (d g) -> p d g", d=4)
                for k in (1, 2, 4):
                    bc = lambda v: v[:, k - 1:k, :].to_broadcast([P, k, G])
                    cmul(pr[:, k:2 * k, :], pi[:, k:2 * k, :], pr[:, 0:k, :], pi[:, 0:k, :], bc(pr), bc(pi), ta[:, 0:k, :], tb[:, 0:k, :])
                zr, zi = r(0), r(1)
                step(TS(r(5), pr[:, 0, :], -1.0, None, ALU.add))
                step(TT(r(3), r(5), ar, ALU.mult))
                step(TT(r(4), pi[:, 0, :], ai, ALU.mult))
                step(TT(r(3), r(3), r(4), ALU.add))
                step(TT(zr, r(3), den, ALU.mult))
                step(TT(r(3), pi[:, 0, :], ar, ALU.mult))
                step(TT(r(4), r(5), ai, ALU.mult))
                step(TT(r(3), r(3), r(4), ALU.subtract))
                step(TT(r(3), r(3), den, ALU.mult))
                step(TS(zi, r(3), sgn, None, ALU.mult))
                wide = lambda v: v.unsqueeze(2).to_broadcast([P, G, GC])
                wA = slot[4][:, 0:D].rearrange("p (g c) -> p g c", g=G)
                wB = slot[4][:, D:2 * D].rearrange("p (g c) -> p g c", g=G)
                pool.wait_ge(gate_ps, 1)
                pool.wait_ge(xT_ready, 4)
                step(TT(wA, BB, wide(zi), ALU.mult))
                step(TT(wB, BA, wide(zi), ALU.mult))
                step(TT(BA, BA, wide(zr), ALU.mult))
                step(TT(BA, BA, wA, ALU.add))
                step(TT(BB, BB, wide(zr), ALU.mult))
                step(TT(BB, BB, wB, ALU.subtract))
                step(TS(slot[1][:, D:2 * D], slot[1][:, D:2 * D], sgn, None, ALU.mult))
                step(TS(slot[3][:, 0:D], slot[3][:, 0:D], nsgn, None, ALU.mult))
                step(TS(slot[3][:, D:2 * D], slot[3][:, D:2 * D], -1.0, None, ALU.mult))
                cmul(r(10), r(11), cs, sn, cs, sn, r(3), r(4))
                cmul(r(0), r(1), r(10), r(11), r(10), r(11), r(3), r(4))
                cmul(prm[:, 0, :], prm[:, 1, :], r(0), r(1), r(0), r(1), r(3), r(4))
                step(TT(r(3), mag, mag, ALU.mult))
                step(TT(r(4), r(3), r(3), ALU.mult))
                step(TT(mag8[:, :], r(4), r(4), ALU.mult))
                nc.gpsimd.memset(slot[4][:, 0:1], 0.0).then_inc(lam_ready, 1)

            def s5_tables():
                prg, pig = (lam[:, i, :, :].rearrange("p d g -> p g d") for i in range(2))
                prb, pib = (lam[:, i, 6::-1, :].rearrange("p d g -> p g d") for i in range(2))
                nb = 16
                tC = slot[4][:, 0:nb * P].rearrange("p (g d c) -> p g d c", g=nb, d=STEP)
                tW = slot[4][:, 0:nb * 7 * GC].rearrange("p (g d c) -> p g d c", g=nb, d=7)
                BTs = BT[:, :, :].rearrange("p g (s c) -> p g s c", s=STEP)
                pool.wait_ge(xT_ready, 8)
                for i in range(GROUPS // nb):
                    gs = slice(i * nb, (i + 1) * nb)
                    pw = lambda v, k: v[:, gs, :].unsqueeze(3).to_broadcast([P, nb, k, GC])
                    cw = lambda v, k: v[:, gs, :].unsqueeze(2).to_broadcast([P, nb, k, GC])
                    step(TT(CT[:, gs, :, :], pw(prg, STEP), cw(CA, STEP), ALU.mult))
                    step(TT(tC, pw(pig, STEP), cw(CB, STEP), ALU.mult))
                    step(TT(CT[:, gs, :, :], CT[:, gs, :, :], tC, ALU.add))
                    step(TT(BTs[:, gs, 0:7, :], pw(prb, 7), cw(BA, 7), ALU.mult))
                    step(TT(tW, pw(pib, 7), cw(BB, 7), ALU.mult))
                    step(TT(BTs[:, gs, 0:7, :], BTs[:, gs, 0:7, :], tW, ALU.add))
                    nc.gpsimd.tensor_copy(BTs[:, gs, 7, :], BA[:, gs, :])
                step(nc.gpsimd.memset(slot[4][:, 0:1], 0.0))
                nc.gpsimd.memset(slot[4][:, 0:1], 0.0).then_inc(tables, 1)

            n = 0
            for l in range(layers):
                kind = MIXERS[l]
                if kind == "fox":
                    if l > 0:
                        pool.wait_ge(x_ready, TM * 2 * l)
                    nc.gpsimd.tensor_copy(
                        qa[HD:KQ, :, :], cst[HD:KQ, C_HOT:C_HOT + HEADS].unsqueeze(2).to_broadcast([HEADS, HEADS, SEQ])
                    ).then_inc(qa_rows, 1)
                    if l == 0 and layers > 1:
                        pool.wait_ge(qa_rows, 1)
                        s5_parameters()
                for k in range(2):
                    if kind == "s5" and k == 0:
                        pool.wait_ge(y_ps, 4)
                    if n > 0:
                        pool.wait_ge(x_ready, TM * n)
                    for q in range(2):
                        pool.dma_start(gb[:, q, :], t["ln_row"][q, n].partition_broadcast(P)).then_inc(gb_landed, 16)
                    if n == 1 and layers > 1:
                        s5_tables()
                    pool.wait_ge(gb_landed, 32 * (n + 1))
                    if n == n_ln - 1:
                        break
                    for m in range(TM):
                        pool.wait_ge(xn_ready, TM * n + m + 1)
                        step(TT(x_tm[:, m, :], res[:, m, :], gb[:, 0, :], ALU.mult))
                        TT(x_tm[:, m, :], x_tm[:, m, :], gb[:, 1, :], ALU.add).then_inc(x_ready, 1)
                    n += 1

        @block.scalar
        def _(act):
            nxt = [0]
            own = [0]

            def step(ins):
                own[0] += 1
                ins.then_inc(act_own, 1)
                act.wait_ge(act_own, own[0])

            def hi(c, k=0):
                act.wait_ge(raw_landed[c % RAW], 16 * (c // RAW + 1) + 16 * k)
                if c >= SPL:
                    act.wait_ge(w_used, c - SPL + 1 + RAW * k)
                nc.scalar.activation(whi[:, c % SPL, :], raw[:, c % RAW, :], ACT.Copy).then_inc(w_hi, 1)

            def hi_to(c):
                while nxt[0] <= min(c, n_tiles - 1):
                    hi(nxt[0])
                    nxt[0] += 1

            def ln(n, nexttile):
                if n >= 0:
                    nc.scalar.preload_act_table(ACT.Sqrt)
                    for m in range(TM):
                        act.wait_ge(var_ready, TM * n + m + 1)
                        nc.scalar.activation(std[:, m, :], mv[:, m, 1:2], ACT.Sqrt, bias=cst[:, C_EPS:C_EPS + 1]).then_inc(std_ready, 1)
                    if n == n_ln - 1:
                        return
                for b in range(4):
                    act.wait_ge(xval_ready, 4 * (n + 1) + b + 1)
                    nc.scalar.activation(xhi[:, 2 * b:2 * b + 2, :], xval[:, b, :].rearrange("p (k t) -> p k t", k=2), ACT.Copy).then_inc(xhi_ready, 1)

            def ffn(l):
                T0 = starts[l] + MIX_TILES[MIXERS[l]]
                E0 = FCH * l

                def chunk(c, k=0, dc=0):
                    t0 = T0 + 3 * c
                    hi(t0 + 2, k)
                    act.wait_ge(w_used, t0 + (0 if c else 1) + RAW * k)
                    nc.scalar.activation(silu[:, :], bank[4][:, 0:SEQ], ACT.Silu).then_inc(silu_ready, 1)
                    hi(t0 + 3, k)
                    act.wait_ge(h_ready, E0 + c + 1 + 2 * k)
                    nc.scalar.activation(hhi[:, c % 2, :], hval[:, :], ACT.Copy).then_inc(hhi_ready, 1)
                    hi(t0 + 4, k)

                hi_to(T0 + 1)
                nc.scalar.preload_act_table(ACT.Silu)
                with act.Fori(0, (FCH - 2) // 2) as k:
                    chunk(0, k)
                    chunk(1, k)
                chunk(FCH - 2)
                c = FCH - 1
                act.wait_ge(w_used, T0 + 3 * c)
                nc.scalar.activation(silu[:, :], bank[4][:, 0:SEQ], ACT.Silu).then_inc(silu_ready, 1)
                act.wait_ge(h_ready, E0 + c + 1)
                nc.scalar.activation(hhi[:, c % 2, :], hval[:, :], ACT.Copy).then_inc(hhi_ready, 1)
                nxt[0] = T0 + T_FFN - 1
                hi_to(T0 + T_FFN + 1)

            def fox(l, f):
                T0 = starts[l]
                hi_to(T0 + 2)
                act.wait_ge(gate_z, f + 1)
                step(nc.scalar.activation(zg[:, 2, :], zg[:, 1, :], ACT.Exp, scale=-1.0))
                nc.scalar.activation(zg[:, 2, :], zg[:, 2, :], ACT.Ln, bias=1.0).then_inc(gate_l, 1)
                for c in range(KC):
                    hi_to(T0 + c + 2)
                for j in range(2):
                    act.wait_ge(w_used, T0 + KC)
                    nc.scalar.copy(vt[:, 0, j * HALF:(j + 1) * HALF], bank[j][:, :]).then_inc(v_sb, 1)
                E1 = PAIRS * f
                E2 = HEADS * f
                for j in range(PAIRS + 2):
                    tq = T0 + KC + 2 * j
                    if j < PAIRS:
                        hi_to(tq + 2)
                    if j < PAIRS:
                        act.wait_ge(w_used, tq + 1)
                        for s in range(2):
                            nc.scalar.copy(qa[0:HD, 2 * j + s, :], bank[4][s * HD:(s + 1) * HD, 0:SEQ]).then_inc(q_sb, 1)
                        hi_to(tq + 3)
                    if j >= 2:
                        for s in range(2):
                            act.wait_ge(pT_ps, E2 + 2 * (j - 2) + s + 1)
                            if j >= 3:
                                act.wait_ge(o_ps, E1 + j - 2)
                            nc.scalar.copy(pT[:, s, :], bank[s][:, 0:3 * P]).then_inc(pT_sb, 1)
                    if 1 <= j <= PAIRS:
                        for s in range(2):
                            act.wait_ge(s_sb, E2 + 2 * (j - 1) + s + 1)
                            nc.scalar.activation(sc[:, s, 0:P], sc[:, s, 0:P], ACT.Exp, scale=0.125,
                                                 bias=smx[:, s, 2:3], accum_out=smx[:, s, 4:5])
                            nc.scalar.activation(sc[:, s, P:3 * P], sc[:, s, P:3 * P], ACT.Exp, scale=0.125,
                                                 bias=smx[:, s, 3:4], accum_out=smx[:, s, 5:6]).then_inc(e_sb, 1)
                    if j >= 2:
                        act.wait_ge(o_ps, E1 + j - 1)
                        nc.scalar.copy(ohi[:, j - 2, :], bank[2 + j % 2][:, 0:SEQ]).then_inc(ohi_sb, 1)
                for c in range(KC):
                    hi_to(T0 + KC + 2 * PAIRS + c + 2)

            def s5(l):
                T0 = starts[l]
                for c in range(KC):
                    hi_to(T0 + c + 2)
                    act.wait_ge(wb_ps, 2 * c + 1)
                    nc.scalar.copy(BT[:, 8 * c:8 * c + 4, :], bank[4 + (2 * c) % 4][:, :].rearrange("p (g n) -> p g n", g=4)).then_inc(bt_sb, 1)
                act.wait_ge(x_ready, TM * 2 * l)
                act.wait_ge(w_used, T0 + KC)
                for j in range(2):
                    nc.scalar.copy(u_tm[:, 0, j * HALF:(j + 1) * HALF], bank[j][:, :]).then_inc(u_sb, 1)
                for b in range(2):
                    act.wait_ge(m_ps, 2 * b + 1)
                    nc.scalar.copy(Msb[:, 8 * b:8 * b + 4, :], bank[4 + 2 * b][:, :].rearrange("p (g n) -> p g n", g=4)).then_inc(m_sb, 1)
                act.wait_ge(m_ps, 4)
                act.wait_ge(u_sb, 4)
                for j in range(4):
                    for m in range(TM):
                        act.dma_start(U2[32 * j + 16 * m:32 * j + 16 * m + 16, :, :], u_tm[:, m, 256 * j:256 * j + 256]).then_inc(u2_ld, 16)
                act.wait_ge(m_d, 1)
                act.wait_ge(zero_st, 16 * 8)
                toep = t["toep"].rearrange("p (g n) -> p g n", g=GROUPS)
                for s in range(STEP):
                    for j in range(4):
                        act.dma_start(toep[s * GC:(s + 1) * GC, 16 * j:16 * j + 16, s * GC:P],
                                      Msb[32 * j:32 * j + GC, :, 0:P - s * GC]).then_inc(m_st, 16)
                act.wait_ge(u2_ld, 16 * 8)
                nc.scalar.copy(Ug[:, 0:8, :, :], U2s[:, 0:8, :, :]).then_inc(ug_sb, 1)
                act.wait_ge(m_st, 16 * 32)
                for j in range(4):
                    act.wait_ge(uT_ps, j + 1)
                    nc.scalar.copy(Ust[:, 16 * j:16 * j + 16, :], bank[4 + j][:, :].rearrange("p (g n) -> p g n", g=16)).then_inc(uT_sb, 1)
                for j in range(4):
                    act.wait_ge(st_ps, j + 1)
                    act.dma_start(BT[:, 16 * j:16 * j + 16, :], t["toep"][:, j * 2 * D:(j + 1) * 2 * D].rearrange("p (g n) -> p g n", g=16)).then_inc(tp_ld[j], 16)
                    nc.scalar.copy(Ssb[:, 16 * j:16 * j + 16, :], bank[j][:, :].rearrange("p (g n) -> p g n", g=16)).then_inc(st_sb, 1)
                ys = slot[3][:, :].rearrange("p (s g c) -> p g s c", s=STEP, g=16)
                for b in range(4):
                    act.wait_ge(y_ps, b + 1)
                    nc.scalar.activation(ys[:, 4 * b:4 * b + 4, :, :], bank[b][:, :].rearrange("p (g s c) -> p g s c", g=4, s=STEP), ACT.Gelu_apprx_tanh).then_inc(y_sb, 1)
                act.wait_ge(y_sb, 4)
                for j in range(4):
                    for m in range(TM):
                        act.dma_start(y_tm[:, m, 256 * j:256 * j + 256], slot[3][32 * j + 16 * m:32 * j + 16 * m + 16, :]).then_inc(yt_ld, 16)
                act.dma_start(bglu, t["b_glu"]).then_inc(bglu_landed, 16)
                for b in range(4):
                    act.wait_ge(yT_ps, b + 1)
                    nc.scalar.copy(ohi[:, 2 * b:2 * b + 2, :], bank[4 + b][:, :].rearrange("p (k t) -> p k t", k=2)).then_inc(yhi_sb, 1)
                for j in range(2):
                    for c in range(KC):
                        hi_to(T0 + KC + j * KC + c + 2)
                    for m in range(TM):
                        if m == 0:
                            act.wait_ge(glu_ps, j + 1)
                        else:
                            act.wait_ge(w_used, T0 + KC + (j + 1) * KC)
                        nc.scalar.activation(slot[1][:, (2 * j + m) * HALF:(2 * j + m + 1) * HALF], bank[4 * j + 2 * m + 1][:, :], ACT.Sigmoid).then_inc(sig_sb, 1)

            def poolmix(l):
                T0 = starts[l]
                act.wait_ge(later_landed, 16 * len(LATER))
                act.wait_ge(pads_zero, 1)
                for c in range(KC):
                    hi_to(T0 + c + 2)
                    act.wait_ge(w_used, T0 + c + 1)
                    if c >= 2:
                        act.wait_ge(pm_sb, c - 1)
                    nc.scalar.copy(ub[c % 2][:, PADT:], bank[c % 2][:, 0:SEQ]).then_inc(pu_sb, 1)
                    if c >= 1:
                        act.wait_ge(pm_sb, c)
                        nc.scalar.copy(ohi[:, c - 1, :], slot[3][:, ((c - 1) % 2) * SEQ:((c - 1) % 2 + 1) * SEQ]).then_inc(phi_sb, 1)
                act.wait_ge(pm_sb, KC)
                nc.scalar.copy(ohi[:, KC - 1, :], slot[3][:, ((KC - 1) % 2) * SEQ:((KC - 1) % 2 + 1) * SEQ]).then_inc(phi_sb, 1)
                for c in range(2):
                    hi_to(T0 + KC + c + 2)
                    for e in range(4):
                        q = 4 * c + e
                        if e < 3:
                            act.wait_ge(pg_ps, 3 * c + e + 1)
                        else:
                            act.wait_ge(w_used, T0 + KC + c + 1)
                        nc.scalar.activation(xhi[:, q, :], bank[4 + q % 4][:, 0:SEQ], ACT.Copy, scale=pscale[:, q:q + 1]).then_inc(zhi_sb, 1)
                for c in range(KC):
                    hi_to(T0 + KC + 2 + c + 2)

            act.wait_ge(small_landed, 16 * len(FIRST))
            if layers > 1:
                act.wait_ge(prm_dve, 1)
                nc.scalar.activation(slot[0][:, 6 * GROUPS:8 * GROUPS], slot[0][:, 4 * GROUPS:6 * GROUPS], ACT.Sin).then_inc(prm_act, 1)
            hi_to(1)
            ln(-1, 0)
            n = 0
            f = 0
            for l in range(layers):
                kind = MIXERS[l]
                if kind == "fox":
                    fox(l, f)
                    f += 1
                elif kind == "s5":
                    s5(l)
                else:
                    poolmix(l)
                ln(n, 0)
                ffn(l)
                ln(n + 1, 0)
                n += 2
            act.wait_ge(x_ready, 2 * (n_ln - 1) + TM)
            act.dma_start(t["out"].rearrange("(m p) d -> p m d", m=TM), x_tm[:, :, :]).then_inc(stored, 16)
            act.wait_ge(stored, 16)

        @block.vector
        def _(dve):
            nxt = [0]
            own = [0]
            V = nc.vector

            def step(ins):
                own[0] += 1
                ins.then_inc(dve_own, 1)
                dve.wait_ge(dve_own, own[0])

            def lo(c, k=0):
                dve.wait_ge(w_hi, c + 1 + RAW * k)
                V.tensor_tensor(wlo[:, c % SPL, :], raw[:, c % RAW, :], whi[:, c % SPL, :].bitcast(F32), ALU.subtract).then_inc(w_lo, 1)

            def lo_to(c):
                while nxt[0] <= min(c, n_tiles - 1):
                    lo(nxt[0])
                    nxt[0] += 1

            def ln(n, last_tile=None, src=None):
                if n >= 0:
                    in_psum = src is None
                    if in_psum:
                        src = lambda m, j: bank[2 * m + j][:, :]
                    if n == 0 and layers > 1:
                        dve.wait_ge(lam_ready, 1)
                    for m in range(TM):
                        if n > 0:
                            dve.wait_ge(x_ready, TM * (n - 1) + m + 1)
                        if n == 0:
                            dve.wait_ge(x_landed, 16)
                        if in_psum and m == 0:
                            dve.wait_ge(sub_done, n + (1 if n < 2 else 0))
                        if in_psum and m == 1:
                            dve.wait_ge(w_used, last_tile + 1)
                        for j in range(2):
                            cols = slice(j * HALF, (j + 1) * HALF)
                            step(V.scalar_tensor_tensor(res[:, m, cols], x_tm[:, m, cols], ALPHA, src(m, j), ALU.mult, ALU.add))
                            ins = V.bn_stats(stats[:, m, j, :], res[:, m, cols])
                        step(ins)
                        V.bn_aggr(mv[:, m, :], stats[:, m, :, :]).then_inc(var_ready, 1)
                    for m in range(TM):
                        dve.wait_ge(std_ready, TM * n + m + 1)
                        step(V.reciprocal(rstd[:, m, :], std[:, m, :]))
                        V.tensor_scalar(res[:, m, :], res[:, m, :], mv[:, m, 0:1], rstd[:, m, :], ALU.subtract, ALU.mult).then_inc(xn_ready, 1)
                    if n == n_ln - 1:
                        dve.wait_ge(gb_landed, 32 * n_ln)
                        for m in range(TM):
                            dve.wait_ge(xn_ready, TM * n + m + 1)
                            step(V.tensor_tensor(x_tm[:, m, :], res[:, m, :], gb[:, 0, :], ALU.mult))
                            V.tensor_tensor(x_tm[:, m, :], x_tm[:, m, :], gb[:, 1, :], ALU.add).then_inc(x_ready, 1)
                        return
                if n == 1 and layers > 1:
                    dve.wait_ge(tables, 1)
                for b in range(4):
                    dve.wait_ge(xnT_ready, 4 * (n + 1) + b + 1)
                    if n < 0:
                        V.tensor_copy(xval[:, b, :], bank[4 + b][:, :]).then_inc(xval_ready, 1)
                    else:
                        for q in range(2):
                            cols = slice(q * SEQ, (q + 1) * SEQ)
                            ins = V.tensor_scalar(xval[:, b, cols], bank[4 + b][:, cols], ln_col[:, 0, n, 2 * b + q:2 * b + q + 1],
                                                  ln_col[:, 1, n, 2 * b + q:2 * b + q + 1], ALU.mult, ALU.add)
                        ins.then_inc(xval_ready, 1)
                    dve.wait_ge(xhi_ready, 4 * (n + 1) + b + 1)
                    V.tensor_tensor(xlo[:, 2 * b:2 * b + 2, :], xval[:, b, :].rearrange("p (k t) -> p k t", k=2),
                                    xhi[:, 2 * b:2 * b + 2, :].bitcast(F32), ALU.subtract).then_inc(xT_ready, 1)

            def ffn(l):
                T0 = starts[l] + MIX_TILES[MIXERS[l]]
                E0 = FCH * l

                def gate(c, k=0):
                    dve.wait_ge(silu_ready, E0 + c + 1 + 2 * k)
                    dve.wait_ge(w_used, T0 + 3 * c + (1 if c else 2) + RAW * k)
                    V.tensor_tensor(hval[:, :], bank[5][:, 0:SEQ], silu[:, :], ALU.mult).then_inc(h_ready, 1)

                def gate_lo(c, k=0):
                    dve.wait_ge(hhi_ready, E0 + c + 1 + 2 * k)
                    V.tensor_tensor(hlo[:, c % 2, :], hval[:, :], hhi[:, c % 2, :].bitcast(F32), ALU.subtract).then_inc(hlo_ready, 1)

                def chunk(c, k=0):
                    t0 = T0 + 3 * c
                    lo(t0 + 2, k)
                    gate(c, k)
                    lo(t0 + 3, k)
                    gate_lo(c, k)
                    lo(t0 + 4, k)
                    dve.wait_ge(hlo_ready, E0 + c + 1 + 2 * k)

                lo_to(T0 + 1)
                with dve.Fori(0, (FCH - 2) // 2) as k:
                    chunk(0, k)
                    chunk(1, k)
                chunk(FCH - 2)
                gate(FCH - 1)
                gate_lo(FCH - 1)
                nxt[0] = T0 + T_FFN - 1
                lo_to(T0 + T_FFN + 1)

            def fox(l, f):
                T0 = starts[l]
                E1, E2 = PAIRS * f, HEADS * f
                lo_to(T0 + 2)
                dve.wait_ge(gate_ps, f + 1)
                step(V.tensor_scalar(zg[:, 0, :], bank[7][0:HEADS, 0:SEQ], bf[:, f:f + 1], None, ALU.add))
                step(V.tensor_scalar(zg[:, 3, :], zg[:, 0, :], -1.0, None, ALU.mult))
                V.tensor_tensor(zg[:, 1, :], zg[:, 0, :], zg[:, 3, :], ALU.max).then_inc(gate_z, 1)
                step(V.tensor_scalar(zg[:, 3, :], zg[:, 3, :], 0.0, 8.0, ALU.max, ALU.mult))
                step(V.memset(ones[:, :], 1.0))
                dve.wait_ge(gate_l, f + 1)
                step(V.scalar_tensor_tensor(zg[:, 1, :], zg[:, 2, :], 8.0, zg[:, 3, :], ALU.mult, ALU.add))
                step(V.tensor_tensor_scan(zg[:, 0, :], ones[:, :], zg[:, 1, :], 0.0, ALU.mult, ALU.add))
                V.tensor_copy(ka[HD:KQ, :, :], zg[:, 0, :].unsqueeze(1).to_broadcast([HEADS, HEADS, SEQ])).then_inc(ka_rows, 1)
                for c in range(KC):
                    lo_to(T0 + c + 2)
                dve.wait_ge(w_used, T0 + KC)
                for j in range(2):
                    V.tensor_copy(vt[:, 1, j * HALF:(j + 1) * HALF], bank[2 + j][:, :]).then_inc(v_sb, 1)
                for j in range(PAIRS + 2):
                    tq = T0 + KC + 2 * j
                    if j < PAIRS:
                        lo_to(tq + 2)
                    if j >= 2:
                        for s in range(2):
                            dve.wait_ge(e_sb, E2 + 2 * (j - 2) + s + 1)
                            step(V.reciprocal(smx[:, s, 6:8], smx[:, s, 4:6]))
                            V.tensor_scalar(sc[:, s, 0:P], sc[:, s, 0:P], smx[:, s, 6:7], None, ALU.mult)
                            V.tensor_scalar(sc[:, s, P:3 * P], sc[:, s, P:3 * P], smx[:, s, 7:8], None, ALU.mult).then_inc(p_sb, 1)
                    if j < PAIRS:
                        dve.wait_ge(w_used, tq + 2)
                        for s in range(2):
                            V.tensor_copy(ka[0:HD, 2 * j + s, :], bank[5][s * HD:(s + 1) * HD, 0:SEQ]).then_inc(k_sb, 1)
                        lo_to(tq + 3)
                    if 1 <= j <= PAIRS:
                        for s in range(2):
                            dve.wait_ge(s_ps, E2 + 2 * (j - 1) + s + 1)
                            if j >= 2:
                                dve.wait_ge(pT_ps, E2 + 2 * (j - 2) + s + 1)
                            V.tensor_tensor_reduce(sc[:, s, 0:P], bank[6 + s][:, 0:P], cst[:, C_MASK + P:C_MASK + 2 * P], 1.0, NEG,
                                                   ALU.add, ALU.max, smx[:, s, 0:1])
                            step(V.tensor_tensor_reduce(sc[:, s, P:3 * P], bank[6 + s][:, P:3 * P], cst[:, C_MASK:C_MASK + 2 * P], 1.0, NEG,
                                                        ALU.add, ALU.max, smx[:, s, 1:2]))
                            V.tensor_scalar(smx[:, s, 2:4], smx[:, s, 0:2], -0.125, None, ALU.mult).then_inc(s_sb, 1)
                    if j >= 2:
                        dve.wait_ge(ohi_sb, E1 + j - 1)
                        V.tensor_tensor(olo[:, j - 2, :], bank[2 + j % 2][:, 0:SEQ], ohi[:, j - 2, :].bitcast(F32), ALU.subtract).then_inc(olo_sb, 1)
                for c in range(KC):
                    lo_to(T0 + KC + 2 * PAIRS + c + 2)

            def vexp(y, x, a, b, ci):
                step(V.tensor_scalar(a, x, 1.4426950408889634, MAGIC, ALU.mult, ALU.add))
                step(V.tensor_scalar(a, a, MAGIC, None, ALU.subtract))
                step(V.tensor_scalar(a, a, -127.0, 128.0, ALU.max, ALU.min))
                step(V.scalar_tensor_tensor(b, a, -LN2_HI, x, ALU.mult, ALU.add))
                step(V.scalar_tensor_tensor(b, a, -LN2_LO, b, ALU.mult, ALU.add))
                step(V.tensor_scalar(ci.bitcast(I32), a, 127.0, float(1 << 23), ALU.add, ALU.mult))
                step(V.tensor_scalar(y, b, EXP_C[0], None, ALU.mult))
                for cf in EXP_C[1:] + [1.0]:
                    step(V.scalar_tensor_tensor(y, y, cf, b, ALU.add, ALU.mult))
                step(V.tensor_scalar(y, y, 1.0, None, ALU.add))
                step(V.tensor_tensor(y, y, ci, ALU.mult))

            def cmul(yr, yi, ar, ai, br, bi, t1, t2):
                step(V.tensor_tensor(t1, ar, br, ALU.mult))
                step(V.tensor_tensor(t2, ai, bi, ALU.mult))
                step(V.tensor_tensor(yr, t1, t2, ALU.subtract))
                step(V.tensor_tensor(t1, ar, bi, ALU.mult))
                step(V.tensor_tensor(t2, ai, br, ALU.mult))
                step(V.tensor_tensor(yi, t1, t2, ALU.add))

            def s5_angles():
                def r(i, n=1):
                    return slot[0][:, i * GROUPS:(i + n) * GROUPS]
                ar, ai, ldt = prm[:, 0, :], prm[:, 1, :], prm[:, 2, :]
                dt, th, den, t1, mag, t2 = r(0), r(1), r(2), r(3), r(8), r(10)
                vexp(dt, ldt, t1, t2, r(9))
                step(V.tensor_tensor(th, ai, dt, ALU.mult))
                step(V.tensor_tensor(r(11), ar, dt, ALU.mult))
                vexp(mag, r(11), t1, t2, r(9))
                step(V.tensor_scalar(t1, th, 1.0 / (2 * np.pi), MAGIC, ALU.mult, ALU.add))
                step(V.tensor_scalar(t1, t1, MAGIC, None, ALU.subtract))
                for cpart in TWO_PI:
                    step(V.scalar_tensor_tensor(th, t1, -cpart, th, ALU.mult, ALU.add))
                step(V.tensor_scalar(r(4), th, np.pi, -np.pi, ALU.min, ALU.max))
                step(V.tensor_scalar(t1, r(4), np.pi / 2, -2 * np.pi, ALU.is_gt, ALU.mult))
                step(V.scalar_tensor_tensor(t2, r(4), np.pi / 2, t1, ALU.add, ALU.add))
                step(V.tensor_scalar(r(5), t2, np.pi, -np.pi, ALU.min, ALU.max))
                step(V.tensor_tensor(t1, ar, ar, ALU.mult))
                step(V.tensor_tensor(t2, ai, ai, ALU.mult))
                step(V.tensor_tensor(t1, t1, t2, ALU.add))
                V.reciprocal(den, t1).then_inc(prm_dve, 1)

            def s5(l):
                T0 = starts[l]
                G = GROUPS
                for c in range(KC):
                    lo_to(T0 + c + 2)
                    dve.wait_ge(wb_ps, 2 * c + 2)
                    V.tensor_copy(BT[:, 8 * c + 4:8 * c + 8, :], bank[5 + (2 * c) % 4][:, :].rearrange("p (g n) -> p g n", g=4)).then_inc(bt_sb2, 1)
                dve.wait_ge(x_ready, TM * 2 * l)
                dve.wait_ge(w_used, T0 + KC)
                for j in range(2):
                    V.tensor_copy(u_tm[:, 1, j * HALF:(j + 1) * HALF], bank[2 + j][:, :]).then_inc(u_sb, 1)
                def r(i):
                    return slot[4][:, i * G:(i + 1) * G]
                a, bq = (prm[:, 0, :], prm[:, 1, :]), (prm[:, 2, :], silu[:, 0:G])
                V.memset(cosT[:, :, 0:1], 1.0)
                step(V.memset(sinT[:, :, 0:1], 0.0))
                k = 1
                for _k in range(5):
                    bc = lambda v: v.unsqueeze(2).to_broadcast([P, G, k])
                    e1 = slot[4][:, 0:G * k].rearrange("p (g n) -> p g n", g=G)
                    e2 = slot[4][:, D:D + G * k].rearrange("p (g n) -> p g n", g=G)
                    cmul(cosT[:, :, k:2 * k], sinT[:, :, k:2 * k], cosT[:, :, 0:k], sinT[:, :, 0:k], bc(a[0]), bc(a[1]), e1, e2)
                    if k < 16:
                        cmul(bq[0], bq[1], a[0], a[1], a[0], a[1], silu[:, G:2 * G], silu[:, 2 * G:3 * G])
                        a, bq = bq, a
                    if k == 4:
                        for b in range(2):
                            dve.wait_ge(m_ps, 2 * b + 2)
                            step(V.tensor_copy(Msb[:, 8 * b + 4:8 * b + 8, :], bank[5 + 2 * b][:, :].rearrange("p (g n) -> p g n", g=4)))
                        tD = hval[:, :].rearrange("p (g c) -> p g c", g=16)
                        step(V.tensor_tensor(tD, dcol[:, :].unsqueeze(2).to_broadcast([P, 16, GC]),
                                             cst[:, C_ID16:C_ID16 + GC].unsqueeze(1).to_broadcast([P, 16, GC]), ALU.mult))
                        dve.wait_ge(m_sb, 2)
                        V.tensor_tensor(Msb[:, :, 0:GC], Msb[:, :, 0:GC], tD, ALU.add).then_inc(m_d, 1)
                    k *= 2
                step(V.tensor_scalar(sinT[:, :, :], sinT[:, :, :], sgn, None, ALU.mult))
                dve.wait_ge(u2_ld, 16 * 8)
                V.tensor_copy(Ug[:, 8:16, :, :], U2s[:, 8:16, :, :]).then_inc(ug_sb, 1)
                dve.wait_ge(uT_ps, 4)
                dec = g3(1)
                step(V.tensor_copy(dec, mag8[:, :].unsqueeze(2).to_broadcast([P, G, NBLK])))
                step(V.memset(dec[:, :, 0:1], 0.0))
                tmp0 = g3(0)
                for j in range(4):
                    q = slice(16 * j, 16 * j + 16)
                    dve.wait_ge(st_sb, j + 1)
                    step(V.tensor_tensor(rot[:, q, :], Ssb[:, q, :], cosT[:, q, :], ALU.mult))
                    dve.wait_ge(sw_ps, j + 1)
                    step(V.tensor_tensor(tmp0[:, q, :], bank[4 + j][:, :].rearrange("p (g n) -> p g n", g=16), sinT[:, q, :], ALU.mult))
                    step(V.tensor_tensor(rot[:, q, :], rot[:, q, :], tmp0[:, q, :], ALU.subtract))
                for j in range(4):
                    c = slice(HALF * j, HALF * (j + 1))
                    V.tensor_tensor_scan(slot[3][:, c], slot[1][:, c], slot[4][:, c], 0.0, ALU.mult, ALU.add).then_inc(g_sb, 1)
                Hs = g3(1)
                dve.wait_ge(g_sb, 4)
                step(V.memset(Hs[:, :, 0:1], 0.0))
                for j in range(4):
                    q = slice(16 * j, 16 * j + 16)
                    step(V.tensor_tensor(rot[:, q, :], Ssb[:, q, :], cosT[:, q, :], ALU.mult))
                    dve.wait_ge(gw_ps, j + 1)
                    step(V.tensor_tensor(tmp0[:, q, :], bank[4 + j][:, :].rearrange("p (g n) -> p g n", g=16), sinT[:, q, :], ALU.mult))
                    V.tensor_tensor(Hs[:, q, 1:NBLK], rot[:, q, 0:NBLK - 1], tmp0[:, q, 0:NBLK - 1], ALU.add).then_inc(hs_sb, 1)
                dve.wait_ge(y_ps, 4)
                step(V.memset(ones_row, 1.0))
                for b in range(4):
                    dve.wait_ge(yhi_sb, b + 1)
                    V.tensor_tensor(olo[:, 2 * b:2 * b + 2, :], bank[4 + b][:, :].rearrange("p (k t) -> p k t", k=2),
                                    ohi[:, 2 * b:2 * b + 2, :].bitcast(F32), ALU.subtract).then_inc(ylo_sb, 1)
                for j in range(2):
                    for c in range(KC):
                        lo_to(T0 + KC + j * KC + c + 2)
                    for m in range(TM):
                        dve.wait_ge(sig_sb, 2 * j + m + 1)
                        q = slice((2 * j + m) * HALF, (2 * j + m + 1) * HALF)
                        ins = V.tensor_tensor(slot[3][:, q], bank[4 * j + 2 * m][:, :], slot[1][:, q], ALU.mult)
                        step(ins)

            def poolmix(l):
                T0 = starts[l]
                V.memset(slot[1][:, 0:6 * 272], 0.0).then_inc(pads_zero, 1)
                dve.wait_ge(pads_zero, 1)
                for c in range(KC):
                    lo_to(T0 + c + 2)
                    w = c // 2
                    u = ub[c % 2]
                    dve.wait_ge(pu_sb, c + 1)
                    s = u
                    off = 0
                    for i in range(w + 1):
                        sh = 1 << i
                        off += sh
                        d = ub[2 + i]
                        step(V.tensor_tensor(d[:, off:], s[:, off:], s[:, off - sh:272 - sh], ALU.add))
                        s = d
                    if c >= 2:
                        dve.wait_ge(plo_sb, c - 1)
                    pm = slot[3][:, (c % 2) * SEQ:(c % 2 + 1) * SEQ]
                    step(V.scalar_tensor_tensor(pm, s[:, PADT:], 1.0 / WINDOWS[w], u[:, PADT:], ALU.mult, ALU.subtract))
                    r = WINDOWS[w] - 1
                    step(V.tensor_tensor(pm[:, 0:r], s[:, PADT:PADT + r], cst[:, C_INV + 16 * w:C_INV + 16 * w + r], ALU.mult))
                    V.tensor_tensor(pm[:, 0:r], pm[:, 0:r], u[:, PADT:PADT + r], ALU.subtract).then_inc(pm_sb, 1)
                    if c >= 1:
                        dve.wait_ge(phi_sb, c)
                        V.tensor_tensor(olo[:, c - 1, :], slot[3][:, ((c - 1) % 2) * SEQ:((c - 1) % 2 + 1) * SEQ], ohi[:, c - 1, :].bitcast(F32), ALU.subtract).then_inc(plo_sb, 1)
                c = KC
                dve.wait_ge(phi_sb, c)
                V.tensor_tensor(olo[:, c - 1, :], slot[3][:, ((c - 1) % 2) * SEQ:((c - 1) % 2 + 1) * SEQ], ohi[:, c - 1, :].bitcast(F32), ALU.subtract).then_inc(plo_sb, 1)
                for c in range(2):
                    lo_to(T0 + KC + c + 2)
                    for e in range(4):
                        q = 4 * c + e
                        dve.wait_ge(zhi_sb, q + 1)
                        V.scalar_tensor_tensor(xlo[:, q, :], bank[4 + q % 4][:, 0:SEQ], pscale[:, q:q + 1], xhi[:, q, :].bitcast(F32), ALU.mult, ALU.subtract).then_inc(zlo_sb, 1)
                for c in range(KC):
                    lo_to(T0 + KC + 2 + c + 2)

            dve.wait_ge(small_landed, 16 * len(FIRST))
            if layers > 1:
                s5_angles()
            lo_to(1)
            ln(-1)
            n = 0
            f = 0
            for l in range(layers):
                kind = MIXERS[l]
                src = None
                if kind == "fox":
                    fox(l, f)
                    f += 1
                elif kind == "s5":
                    s5(l)
                    src = lambda m, j: slot[3][:, (2 * j + m) * HALF:(2 * j + m + 1) * HALF]
                else:
                    poolmix(l)
                ln(n, starts[l] + MIX_TILES[kind] - 1, src)
                ffn(l)
                ln(n + 1, starts[l] + MIX_TILES[kind] + T_FFN - 1)
                n += 2

        @block.tensor
        def _(pe):
            mm = nc.tensor.matmul

            def fm(c, k, dst, bhi, blo, chunks=None, w_at=None, last=True):
                chunks = list(range(KC)) if chunks is None else chunks
                w_at = (lambda i: slice(i * P, (i + 1) * P)) if w_at is None else w_at
                s = c % SPL
                for i, kc in enumerate(chunks):
                    wh, wl = whi[:, s, w_at(i)], wlo[:, s, w_at(i)]
                    mm(dst, wh, bhi[:, kc, :], start=(i == 0), stop=False)
                    mm(dst, wh, blo[:, kc, :], start=False, stop=False)
                    ins = mm(dst, wl, bhi[:, kc, :], start=False, stop=(i == len(chunks) - 1))
                return ins

            def tm(c, a_hi, a_lo, banks, first, last, done=None):
                s = c % SPL
                for m in range(TM):
                    cols = slice(m * P, (m + 1) * P)
                    for j in range(2):
                        mm(banks[2 * m + j][:, :], a_hi[:, cols], whi[:, s, j * HALF:(j + 1) * HALF], start=first, stop=False)
                    for j in range(2):
                        mm(banks[2 * m + j][:, :], a_hi[:, cols], wlo[:, s, j * HALF:(j + 1) * HALF], start=False, stop=False)
                    for j in range(2):
                        ins = mm(banks[2 * m + j][:, :], a_lo[:, cols], whi[:, s, j * HALF:(j + 1) * HALF], start=False, stop=last)
                    if done is not None:
                        done(m, ins)
                return ins

            def used(ins):
                ins.then_inc(w_used, 1)

            def lnT(n, src):
                for b in range(4):
                    for q in range(2):
                        for m in range(TM):
                            if b == 0 and q == 0 and n >= 0:
                                pe.wait_ge(xn_ready, TM * n + m + 1)
                            ins = nc.tensor.transpose(bank[4 + b][:, q * SEQ + m * P:q * SEQ + (m + 1) * P],
                                                      src[:, m, (2 * b + q) * P:(2 * b + q + 1) * P], ident)
                    ins.then_inc(xnT_ready, 1)

            def sub(n):
                def done(m, ins):
                    if m == 0:
                        ins.then_inc(sub_done, 1)
                return done

            def ffn(l, n):
                T0 = starts[l] + MIX_TILES[MIXERS[l]]
                E0 = FCH * l
                acc = bank[0:4]

                def up(c, k=0, first=False):
                    t0 = T0 + (3 * c - 1 if not first else 0)
                    pe.wait_ge(w_lo, t0 + 1 + RAW * k)
                    if E0 + c >= 1:
                        pe.wait_ge(silu_ready, E0 + c + 2 * k)
                    if first:
                        pe.wait_ge(xT_ready, 4 * (n + 1))
                    ins = fm(t0, k, bank[4][:, 0:SEQ], xhi, xlo)
                    used(ins)
                    pe.wait_ge(w_lo, t0 + 2 + RAW * k)
                    if E0 + c >= 1:
                        pe.wait_ge(h_ready, E0 + c + 2 * k)
                    ins = fm(t0 + 1, k, bank[5][:, 0:SEQ], xhi, xlo)
                    used(ins)

                def down(c, k=0, t=None, first=False, last=False):
                    t = T0 + 3 * c + 4 if t is None else t
                    pe.wait_ge(w_lo, t + 1 + RAW * k)
                    pe.wait_ge(hlo_ready, E0 + c + 1 + 2 * k)
                    ins = tm(t, hhi[:, c % 2, :], hlo[:, c % 2, :], acc, first, last, sub(n) if last else None)
                    used(ins)

                up(0, first=True)
                up(1)
                down(0, first=True)
                up(2)
                down(1)
                with pe.Fori(0, (FCH - 4) // 2) as k:
                    up(3, k)
                    down(2, k)
                    up(4, k)
                    down(3, k)
                up(FCH - 1)
                down(FCH - 2)
                down(FCH - 1, t=T0 + T_FFN - 1, last=True)

            def fox(l, f, n):
                T0 = starts[l]
                E1, E2 = PAIRS * f, HEADS * f
                pe.wait_ge(xT_ready, 4 * (n + 1) )
                for kc in range(KC):
                    ins = mm(bank[7][0:HEADS, 0:SEQ], wf[:, f, kc, :], xval[:, kc // 2, (kc % 2) * SEQ:(kc % 2 + 1) * SEQ], start=(kc == 0), stop=(kc == KC - 1))
                ins.then_inc(gate_ps, 1)
                for c in range(KC):
                    pe.wait_ge(w_lo, T0 + c + 1)
                    ins = tm(T0 + c, xhi[:, c, :], xlo[:, c, :], bank[0:4], c == 0, c == KC - 1)
                    used(ins)
                for j in range(PAIRS + 2):
                    tq = T0 + KC + 2 * j
                    if j < PAIRS:
                        pe.wait_ge(w_lo, tq + 1)
                        if j >= 1:
                            pe.wait_ge(q_sb, 2 * (E1 + j))
                        ins = fm(tq, 0, bank[4][:, 0:SEQ], xhi, xlo)
                        used(ins)
                        pe.wait_ge(w_lo, tq + 2)
                        if j >= 1:
                            pe.wait_ge(k_sb, 2 * (E1 + j))
                        ins = fm(tq + 1, 0, bank[5][:, 0:SEQ], xhi, xlo)
                        used(ins)
                    if j >= 2:
                        for s in range(2):
                            pe.wait_ge(p_sb, E2 + 2 * (j - 2) + s + 1)
                            if j == 2:
                                pe.wait_ge(v_sb, 4 * (f + 1))
                            else:
                                pe.wait_ge(pT_sb, E2 + 2 * (j - 3) + s + 1)
                            for b in range(3):
                                ins = nc.tensor.transpose(bank[s][:, b * P:(b + 1) * P], sc[:, s, b * P:(b + 1) * P], ident)
                            ins.then_inc(pT_ps, 1)
                    if 1 <= j <= PAIRS:
                        if j == 1:
                            pe.wait_ge(ka_rows, f + 1)
                            pe.wait_ge(qa_rows, f + 1)
                        pe.wait_ge(q_sb, 2 * (E1 + j))
                        pe.wait_ge(k_sb, 2 * (E1 + j))
                        for s in range(2):
                            h = 2 * (j - 1) + s
                            if j >= 2:
                                pe.wait_ge(s_sb, E2 + 2 * (j - 2) + s + 1)
                            mm(bank[6 + s][:, 0:P], qa[:, h, 0:P], ka[:, h, 0:P], start=True, stop=True)
                            mm(bank[6 + s][:, P:3 * P], qa[:, h, P:SEQ], ka[:, h, :], start=True, stop=True).then_inc(s_ps, 1)
                    if j >= 2:
                        o = bank[2 + j % 2]
                        if j >= 4:
                            pe.wait_ge(olo_sb, E1 + j - 3)
                        for s in range(2):
                            h = 2 * (j - 2) + s
                            pe.wait_ge(pT_sb, E2 + h + 1)
                            dst = slice(s * HD, (s + 1) * HD)
                            mm(o[dst, 0:SEQ], vt[:, 0, h * HD:(h + 1) * HD], pT[:, s, 0:SEQ], start=True, stop=False)
                            ins = mm(o[dst, P:SEQ], vt[:, 1, h * HD:(h + 1) * HD], pT[:, s, SEQ:3 * P], start=False, stop=True)
                        ins.then_inc(o_ps, 1)
                T1 = T0 + KC + 2 * PAIRS
                pe.wait_ge(olo_sb, E1 + PAIRS)
                for c in range(KC):
                    pe.wait_ge(w_lo, T1 + c + 1)
                    ins = tm(T1 + c, ohi[:, c, :], olo[:, c, :], bank[0:4], c == 0, c == KC - 1, sub(n) if c == KC - 1 else None)
                    used(ins)

            def s5(l, n):
                T0 = starts[l]
                pe.wait_ge(xT_ready, 4 * (n + 1))
                pe.wait_ge(tables, 1)
                for c in range(KC):
                    pe.wait_ge(w_lo, T0 + c + 1)
                    used(tm(T0 + c, xhi[:, c, :], xlo[:, c, :], bank[0:4], c == 0, c == KC - 1))
                    for i in range(2):
                        if c >= 2:
                            pe.wait_ge((bt_sb, bt_sb2)[i], c - 1)
                        for g in range(4):
                            ins = nc.tensor.transpose(bank[4 + (2 * c + i) % 4][:, g * P:(g + 1) * P], BT[:, 8 * c + 4 * i + g, :], ident)
                        ins.then_inc(wb_ps, 1)
                pe.wait_ge(bt_sb, KC)
                pe.wait_ge(bt_sb2, KC)
                for b in range(4):
                    for q in range(4):
                        for j in range(4):
                            g = 16 * j + 4 * b + q
                            lhs = slot[1][:, g * GC:g * GC + 32]
                            mm(bank[4 + b][32 * j:32 * j + 32, q * P:q * P + GC], lhs, CA[:, g, :], start=True, stop=True)
                            ins = mm(bank[4 + b][32 * j:32 * j + 32, q * P + GC:(q + 1) * P], lhs,
                                     CT[:, g, 0:STEP - 1, :].rearrange("p d c -> p (d c)"), start=True, stop=True)
                    ins.then_inc(m_ps, 1)
                pe.wait_ge(ug_sb, 2)
                pe.wait_ge(m_d, 1)
                for j in range(4):
                    for g in range(16):
                        ins = nc.tensor.transpose(bank[4 + j][:, g * NBLK:(g + 1) * NBLK], slot[0][32 * j:32 * j + 32, g * P:(g + 1) * P],
                                                  cst[32 * j:32 * j + 32, C_ID + 32 * j:C_ID + 32 * j + 32])
                    ins.then_inc(uT_ps, 1)
                for j in range(4):
                    pe.wait_ge(uT_sb, j + 1)
                    for g in range(16):
                        ins = mm(bank[j][:, g * NBLK:(g + 1) * NBLK], BT[:, 16 * j + g, :], Ust[:, 16 * j + g, :], start=True, stop=True)
                    ins.then_inc(st_ps, 1)
                perm = cst[:, C_PERM:C_PERM + P]
                for j in range(4):
                    pe.wait_ge(st_sb, j + 1)
                    mm(bank[4 + j][:, :], perm, slot[3][:, j * HALF:(j + 1) * HALF], start=True, stop=True).then_inc(sw_ps, 1)
                pe.wait_ge(st_sb, 4)

                def y_at(g):
                    j, b, q = g // 16, g % 16 // 4, g % 4
                    return bank[b][32 * j:32 * j + 32, q * P:(q + 1) * P], (0, 32 * j)
                for g in range(GROUPS):
                    if g % 16 == 0:
                        pe.wait_ge(tp_ld[g // 16], 16)
                    dst, pos = y_at(g)
                    mm(dst, Ust[:, g, :], BT[:, g, :], start=(g % 4 == 0), stop=False, tile_position=pos, skip_group_check=True)
                for j in range(4):
                    pe.wait_ge(g_sb, 4)
                    mm(bank[4 + j][:, :], perm, slot[3][:, j * HALF:(j + 1) * HALF], start=True, stop=True).then_inc(gw_ps, 1)
                pe.wait_ge(hs_sb, 4)
                for b in range(4):
                    for q in range(4):
                        for j in range(4):
                            g = 16 * j + 4 * b + q
                            dst, pos = y_at(g)
                            ins = mm(dst, slot[1][:, g * NBLK:(g + 1) * NBLK], CT[:, g, :, :].rearrange("p d c -> p (d c)"),
                                     start=False, stop=True, tile_position=pos, skip_group_check=True)
                    ins.then_inc(y_ps, 1)
                pe.wait_ge(yt_ld, 16 * 8)
                for b in range(4):
                    for q in range(2):
                        for m in range(TM):
                            ins = nc.tensor.transpose(bank[4 + b][:, q * SEQ + m * P:q * SEQ + (m + 1) * P], y_tm[:, m, (2 * b + q) * P:(2 * b + q + 1) * P], ident)
                    ins.then_inc(yT_ps, 1)
                T1 = T0 + KC
                pe.wait_ge(ylo_sb, 4)
                pe.wait_ge(bglu_landed, 16)
                for j in range(2):
                    banks = bank[4 * j:4 * j + 4]
                    for m in range(TM):
                        for v in range(2):
                            mm(banks[2 * m + v][:, :], ones_row, bglu[:, v * D + j * HALF:v * D + (j + 1) * HALF], start=True, stop=False)
                    for c in range(KC):
                        pe.wait_ge(w_lo, T1 + j * KC + c + 1)

                        def done(m, ins):
                            if m == 0:
                                ins.then_inc(glu_ps, 1)
                        ins = tm(T1 + j * KC + c, ohi[:, c, :], olo[:, c, :], banks, False, c == KC - 1, done if c == KC - 1 else None)
                        used(ins)

            def poolmix(l, n):
                T0 = starts[l]
                pe.wait_ge(xT_ready, 4 * (n + 1))
                for c in range(KC):
                    pe.wait_ge(w_lo, T0 + c + 1)
                    if c >= 2:
                        pe.wait_ge(pu_sb, c - 1)
                    ins = fm(T0 + c, 0, bank[c % 2][:, 0:SEQ], xhi, xlo)
                    used(ins)
                T1 = T0 + KC
                for c in range(2):
                    pe.wait_ge(w_lo, T1 + c + 1)
                    for gl in range(2):
                        gi = 2 * c + gl
                        pe.wait_ge(plo_sb, 2 * gi + 2)
                        for e in range(2):
                            q = 2 * gi + e
                            if q >= 4:
                                pe.wait_ge(zlo_sb, q - 3)
                            ins = fm(T1 + c, 0, bank[4 + q % 4][:, 0:SEQ], ohi, olo, chunks=[2 * gi, 2 * gi + 1],
                                     w_at=lambda i: slice((gl * 4 + i * 2 + e) * P, (gl * 4 + i * 2 + e + 1) * P))
                            if gl == 1 and e == 1:
                                used(ins)
                            else:
                                ins.then_inc(pg_ps, 1)
                T2 = T1 + 2
                pe.wait_ge(zlo_sb, KC)
                for c in range(KC):
                    pe.wait_ge(w_lo, T2 + c + 1)
                    ins = tm(T2 + c, xhi[:, c, :], xlo[:, c, :], bank[0:4], c == 0, c == KC - 1, sub(n) if c == KC - 1 else None)
                    used(ins)

            pe.wait_ge(small_landed, 16 * len(FIRST))
            pe.wait_ge(x_landed, 16)
            lnT(-1, x_tm)
            n = 0
            f = 0
            for l in range(layers):
                kind = MIXERS[l]
                if kind == "fox":
                    fox(l, f, n)
                    f += 1
                elif kind == "s5":
                    s5(l, n)
                else:
                    poolmix(l, n)
                lnT(n, res)
                ffn(l, n + 1)
                if n + 1 < n_ln - 1:
                    lnT(n + 1, res)
                n += 2


def _pack(w):
    tiles = []

    def fm(a, c):
        tiles.append(a[:, c * P:(c + 1) * P].reshape(KC, P, P).transpose(1, 0, 2).reshape(P, D))

    def tm(a, kc):
        tiles.append(a[kc * P:(kc + 1) * P, :])

    seen = {"fox": 0, "s5": 0, "pool": 0}
    for l, kind in enumerate(MIXERS):
        i = seen[kind]
        seen[kind] += 1
        if kind == "fox":
            qkv = w["fox_w_qkv"][i]
            for kc in range(KC):
                tm(qkv[:, 2 * D:], kc)
            for j in range(PAIRS):
                fm(qkv[:, 0:D], j)
                fm(qkv[:, D:2 * D], j)
            for kc in range(KC):
                tm(w["fox_w_o"][i], kc)
        elif kind == "s5":
            for kc in range(KC):
                tm(w["s5_w_in"][i], kc)
            for j in range(2):
                for kc in range(KC):
                    rows = w["s5_w_glu"][i][kc * P:(kc + 1) * P]
                    tiles.append(np.concatenate([rows[:, j * HALF:(j + 1) * HALF], rows[:, D + j * HALF:D + (j + 1) * HALF]], 1))
        else:
            for c in range(KC):
                fm(w["pool_w_in"][i], c)
            for c in range(2):
                g = w["pool_w_grp"][i][2 * c:2 * c + 2].reshape(2, 2, P, 2, P)
                tiles.append(g.transpose(2, 0, 1, 3, 4).reshape(P, D))
            for kc in range(KC):
                tm(w["pool_w_out"][i], kc)
        w1, w3, w2 = w["ffn_w1"][l], w["ffn_w3"][l], w["ffn_w2"][l]
        for c in range(FCH + 1):
            if c < FCH:
                fm(w1, c)
                fm(w3, c)
            if c >= 1:
                tm(w2, c - 1)
    return np.stack(tiles)


def kernel(**inputs):
    import concourse.bacc as bacc
    from concourse.bass_utils import run_bass_kernel_spmd

    w = {k: np.asarray(v) for k, v in inputs.items()}

    def col(a):
        return np.ascontiguousarray(np.moveaxis(a.reshape(*a.shape[:-1], KC, P), -1, 0))

    def state_rows(top, bottom):
        return np.concatenate([top.swapaxes(0, 1), bottom.swapaxes(0, 1)], 0)

    are, aim, ldt = w["s5_a_re"][0], w["s5_a_im"][0], w["s5_log_dt"][0]
    br, bi = w["s5_b_re"][0], w["s5_b_im"][0]
    cr, ci = (w[k][0].transpose(0, 2, 1) for k in ("s5_c_re", "s5_c_im"))
    ldt = np.broadcast_to(ldt[:, None], are.shape)
    dcol = np.zeros((4, 2, GC, 16), np.float32)
    dcol[:, 0] = w["s5_d"][0].reshape(4, 16, GC).transpose(0, 2, 1)
    arrays = {
        "x": w["x"][0],
        "w": _pack(w),
        "consts": constants(),
        "ln_col": col(np.stack([w["ln_g"].reshape(2 * DEPTH, D), w["ln_b"].reshape(2 * DEPTH, D)])),
        "ln_row": np.stack([w["ln_g"].reshape(2 * DEPTH, D), w["ln_b"].reshape(2 * DEPTH, D)]),
        "wf": w["fox_w_f"].reshape(2, KC, P, HEADS).transpose(2, 0, 1, 3),
        "bf": w["fox_b_f"].T,
        "s5_prm": np.stack([state_rows(v, v) for v in (are, aim, ldt)], 1),
        "s5_dcol": dcol.reshape(P, 16),
        "s5_B": np.stack([state_rows(br, bi), state_rows(bi, br)], 1).reshape(P, 2 * D),
        "s5_C": np.stack([state_rows(cr, ci), state_rows(ci, cr)], 1).reshape(P, 2 * D),
        "pool_scale": col(w["pool_scale"][0]),
        "b_glu": w["s5_b_glu"],
    }
    nc = bacc.Bacc("TRN2", target_bir_lowering=False, num_devices=1)
    in_map, t = {}, {}
    for name, a in arrays.items():
        a = np.ascontiguousarray(a)
        in_map[f"in_{name}"] = a
        t[name] = nc.dram_tensor(f"in_{name}", a.shape, mybir.dt.from_np(a.dtype), kind="ExternalInput").ap()
    t["toep"] = nc.dram_tensor("toep", (P, GROUPS * P), F32, kind="Internal").ap()
    t["out"] = nc.dram_tensor("out", (SEQ, D), F32, kind="ExternalOutput").ap()
    build(nc, t)
    r = run_bass_kernel_spmd(nc, [in_map], core_ids=[0])
    return r.results[0]["out"].reshape(1, SEQ, D)
```

```python
from contextlib import ExitStack

import numpy as np

import concourse.bass as bass
from concourse import mybir

F32 = mybir.dt.float32
F32R = mybir.dt.float32r
I32 = mybir.dt.int32
ALU = mybir.AluOpType
ACT = mybir.ActivationFunctionType
AX_X = mybir.AxisListType.X

P = 128
SEQ = 256
D = 1024
KC = D // P
TM = SEQ // P
HALF = 512
DEPTH = 4
D_FF = 2816
FCH = D_FF // P
HEADS, HD = 16, 64
PAIRS = HEADS // 2
GROUPS, GC, ST = 64, 16, 64
STEP = P // GC
NBLK = SEQ // STEP
WINDOWS = (2, 4, 8, 16)
ALPHA = (2.0 * DEPTH) ** 0.25
LN_EPS = 1e-5
NEG = -1.0e30

RAW = 6
SPL = 3

T_FOX = KC + 2 * PAIRS + KC
T_S5 = KC + 2 * KC
T_POOL = KC + 2 + KC
T_FFN = 3 * FCH
MIXERS = ("fox", "s5", "pool", "fox")
MIX_TILES = {"fox": T_FOX, "s5": T_S5, "pool": T_POOL}

C_ID = 0
C_PERM = C_ID + P
C_MASK = C_PERM + P
C_HOT = C_MASK + 2 * P
C_SGN = C_HOT + HEADS
C_NSGN = C_SGN + 1
C_EPS = C_NSGN + 1
C_ID16 = C_EPS + 1
C_INV = C_ID16 + GC
C_N = C_INV + 4 * 16

EXP_C = [1 / 5040, 1 / 720, 1 / 120, 1 / 24, 1 / 6, 0.5]
LN2_HI, LN2_LO = 0.693145751953125, 1.42860677e-06
TWO_PI = (6.28125, 0.0019350051879882812, 3.019916e-07)
MAGIC = 12582912.0


def constants():
    c = np.zeros((P, C_N), np.float32)
    i = np.arange(P)
    c[:, C_ID:C_ID + P] = np.eye(P)
    c[i, C_PERM + (i + ST) % P] = 1.0
    tri = np.where(i[None, :] <= i[:, None], 0.0, NEG)
    c[:, C_MASK + P:C_MASK + 2 * P] = tri
    c[HD:HD + HEADS, C_HOT:C_HOT + HEADS] = np.eye(HEADS)
    c[:, C_SGN] = np.where(i < ST, -1.0, 1.0)
    c[:, C_NSGN] = -c[:, C_SGN]
    c[:, C_EPS] = LN_EPS
    c[i, C_ID16 + i % GC] = 1.0
    for w, win in enumerate(WINDOWS):
        c[:, C_INV + 16 * w:C_INV + 16 * w + 16] = 1.0 / np.minimum(np.arange(1, 17), win)
    return c


def build(nc, t, layers=DEPTH, last_ffn=True):
    starts = []
    at = 0
    for l in range(layers):
        starts.append(at)
        at += MIX_TILES[MIXERS[l]] + T_FFN
    n_tiles = at
    n_ln = 2 * layers

    with ExitStack() as ctx:
        def sb(name, shape, dt=F32):
            return ctx.enter_context(nc.sbuf_tensor(name, shape, dt))

        def sem(name):
            return ctx.enter_context(nc.semaphore(name))

        bank = [ctx.enter_context(nc.psum_tensor(f"bank{i}", [P, HALF], F32)) for i in range(8)]

        cst = sb("cst", [P, C_N])
        raw = sb("raw", [P, RAW, D])
        whi = sb("whi", [P, SPL, D], F32R)
        wlo = sb("wlo", [P, SPL, D], F32R)
        x_tm = sb("x_tm", [P, TM, D])
        xhi = sb("xhi", [P, KC, SEQ], F32R)
        xlo = sb("xlo", [P, KC, SEQ], F32R)
        silu = sb("silu", [P, SEQ])
        hval = sb("hval", [P, SEQ])
        hhi = sb("hhi", [P, 2, SEQ], F32R)
        hlo = sb("hlo", [P, 2, SEQ], F32R)
        ln_col = sb("ln_col", [P, 2, 2 * DEPTH, KC])
        stats = sb("stats", [P, TM, 2, 6])
        mv = sb("mv", [P, TM, 2])
        std = sb("std", [P, TM, 1])
        rstd = sb("rstd", [P, TM, 1])
        nmr = sb("nmr", [P, 1])
        slot = [sb(f"slot{i}", [P, 2 * D]) for i in range(5)]
        smx = sb("smx", [P, 2, 8])
        wf = sb("wf", [P, 2, KC, HEADS])
        bf = sb("bf", [HEADS, 2])
        prm = sb("prm", [P, 3, GROUPS])
        dcol = sb("dcol", [P, 16])
        lam = sb("lam", [P, 2, STEP, GROUPS])
        pscale = sb("pscale", [P, KC])
        mag8 = sb("mag8", [P, GROUPS])
        turn = sb("turn", [P, GROUPS])

        def overlay(*specs):
            with ExitStack() as inner:
                return [inner.enter_context(nc.sbuf_tensor(n, s, d)) for n, s, d in specs]

        KQ = HD + HEADS
        ohi, olo = overlay(("ohi", [P, KC, SEQ], F32R), ("olo", [P, KC, SEQ], F32R))
        cosT, sinT = overlay(("cosT", [P, GROUPS, NBLK], F32), ("sinT", [P, GROUPS, NBLK], F32))
        sb("held", [P, 2 * KC * SEQ])
        qa, ka, vt, sc, pT, zg, ones = overlay(
            ("qa", [KQ, HEADS, SEQ], F32), ("ka", [KQ, HEADS, SEQ], F32), ("vt", [P, TM, D], F32),
            ("sc", [P, 2, 3 * P], F32), ("pT", [P, 2, 3 * P], F32), ("zg", [HEADS, 4, SEQ], F32), ("ones", [HEADS, SEQ], F32))
        BT = sb("BT", [P, GROUPS, P])
        CT = sb("CT", [P, GROUPS, STEP, GC])
        ones_row = CT[0:1, 0, :, :].rearrange("p d c -> p (d c)")
        bglu = BT[0:1, 0:16, :].rearrange("p g n -> p (g n)")

        res = slot[0][:, :].rearrange("p (m d) -> p m d", m=TM)
        xval = slot[4][:, :].rearrange("p (b c) -> p b c", b=4)
        gb = slot[2][:, :].rearrange("p (k d) -> p k d", k=2)

        raw_landed = [sem(f"raw_landed{i}") for i in range(RAW)]
        w_hi, w_lo, w_used = sem("w_hi"), sem("w_lo"), sem("w_used")
        small_landed = sem("small_landed")
        later_landed, x_landed, bglu_landed = sem("later_landed"), sem("x_landed"), sem("bglu_landed")
        ones_set = sem("ones_set")
        sub_done = sem("sub_done")
        var_ready, std_ready, rstd_ready = sem("var_ready"), sem("std_ready"), sem("rstd_ready")
        xn_ready = [sem("xn0_ready"), sem("xn1_ready")]
        xval_ready = [sem("xval_dve"), sem("xval_act")]
        xnT_ready, xhi_ready, xT_ready = sem("xnT_ready"), sem("xhi_ready"), sem("xT_ready")
        gb_landed, x_ready = sem("gb_landed"), sem("x_ready")
        silu_ready = sem("silu_ready")
        h_ready, hhi_ready, hlo_ready = sem("h_ready"), sem("hhi_ready"), sem("hlo_ready")
        dve_own, act_own, pool_own = sem("dve_own"), sem("act_own"), sem("pool_own")
        stored = sem("stored")
        gate_ps, gate_z, gate_l, ka_rows, qa_rows = sem("gate_ps"), sem("gate_z"), sem("gate_l"), sem("ka_rows"), sem("qa_rows")
        v_sb, q_sb, k_sb = sem("v_sb"), sem("q_sb"), sem("k_sb")
        s_ps, s_sb, e_sb, p_sb = sem("s_ps"), sem("s_sb"), sem("e_sb"), sem("p_sb")
        pT_ps, pT_sb, o_ps, ohi_sb, olo_sb = sem("pT_ps"), sem("pT_sb"), sem("o_ps"), sem("ohi_sb"), sem("olo_sb")
        prm_act, prm_dve = sem("prm_act"), sem("prm_dve")
        lam_ready = sem("lam_ready")
        wb_ps, bt_sb, bt_sb2, m_ps, m_sb, m_sb2, m_d, m_st, zero_st, tables = (
            sem(n) for n in ("wb_ps", "bt_sb", "bt_sb2", "m_ps", "m_sb", "m_sb2", "m_d", "m_st", "zero_st", "tables"))
        ug_sb = sem("ug_sb")
        tp_ld = [sem(f"tp_ld{j}") for j in range(4)]
        u_sb, u2_ld, uT_ps, uT_sb = sem("u_sb"), sem("u2_ld"), sem("uT_ps"), sem("uT_sb")
        st_ps, st_sb, sw_ps, rot_sb, g_sb, gw_ps, hs_sb = (sem(n) for n in ("st_ps", "st_sb", "sw_ps", "rot_sb", "g_sb", "gw_ps", "hs_sb"))
        y_ps, y_sb, yt_ld, yT_ps, yhi_sb, ylo_sb = (sem(n) for n in ("y_ps", "y_sb", "yt_ld", "yT_ps", "yhi_sb", "ylo_sb"))
        glu_ps, sig_sb = sem("glu_ps"), sem("sig_sb")
        pads_zero = sem("pads_zero")
        pu_sb, pm_sb, phi_sb, plo_sb = sem("pu_sb"), sem("pm_sb"), sem("phi_sb"), sem("plo_sb")
        pg_ps, zhi_sb, zlo_sb = sem("pg_ps"), sem("zhi_sb"), sem("zlo_sb")

        ident = cst[:, C_ID:C_ID + P]
        sgn = cst[:, C_SGN:C_SGN + 1]
        nsgn = cst[:, C_NSGN:C_NSGN + 1]

        def g3(s, a=0, n=GROUPS, w=NBLK):
            return slot[s][:, a:a + n * w].rearrange("p (g n) -> p g n", g=n)
        u_tm = slot[0][:, :].rearrange("p (m d) -> p m d", m=TM)
        U2 = slot[4][:, :].rearrange("p (s c) -> p s c", s=STEP)
        Msb = slot[2][:, :].rearrange("p (g n) -> p g n", g=16)
        U2s = slot[4][:, :].rearrange("p (s g c) -> p g s c", s=STEP, g=16)
        Ug = slot[0][:, :].rearrange("p (g s c) -> p g s c", g=16, s=STEP)
        Ust, Ssb, rot = g3(2), g3(3), g3(4)
        BA, BB = (slot[1][:, i * D:(i + 1) * D].rearrange("p (g c) -> p g c", g=GROUPS) for i in range(2))
        CA, CB = (slot[3][:, i * D:(i + 1) * D].rearrange("p (g c) -> p g c", g=GROUPS) for i in range(2))
        y_tm = slot[4][:, :].rearrange("p (m d) -> p m d", m=TM)

        PADT = 16
        ub = [slot[1][:, i * 272:(i + 1) * 272] for i in range(6)]

        FIRST = [(cst[:, :], t["consts"]), (ln_col[:, :, :, :], t["ln_col"]), (wf[:, :, :, :], t["wf"]), (bf[:, :], t["bf"]),
                 (prm[:, :, :], t["s5_prm"])]
        LATER = [(dcol[:, :], t["s5_dcol"]), (slot[1][:, :], t["s5_B"]), (slot[3][:, :], t["s5_C"]),
                 (pscale[:, :], t["pool_scale"])]

        ctx.enter_context(nc.allow_low_precision(reason="float32r halves of float32 values"))
        block = ctx.enter_context(nc.Block())

        @block.sync
        def _(sp):
            sp.dma_start(x_tm[:, :, :], t["x"].rearrange("(m p) d -> p m d", m=TM)).then_inc(x_landed, 16)
            for dst, src in FIRST:
                sp.dma_start(dst, src).then_inc(small_landed, 16)
            for c in range(RAW):
                sp.dma_start(raw[:, c, :], t["w"][c]).then_inc(raw_landed[c], 16)
            for dst, src in LATER:
                sp.dma_start(dst, src).then_inc(later_landed, 16)
            rounds = n_tiles // RAW
            with sp.Fori(1, rounds) as i:
                for c in range(RAW):
                    sp.wait_ge(w_lo, RAW * i + (c + 1 - RAW))
                    sp.dma_start(raw[:, c, :], t["w"][RAW * i + c]).then_inc(raw_landed[c], 16)
            for c in range(n_tiles - rounds * RAW):
                sp.wait_ge(w_lo, RAW * (rounds - 1) + c + 1)
                sp.dma_start(raw[:, c, :], t["w"][RAW * rounds + c]).then_inc(raw_landed[c], 16)

        @block.gpsimd
        def _(pool):
            pool.wait_ge(small_landed, 16 * len(FIRST))
            if layers > 1:
                nc.gpsimd.memset(slot[2][:, 0:D], 0.0).then_inc(pool_own, 1)
                pool.wait_ge(pool_own, 1)
                for k in range(8):
                    pool.dma_start(t["toep"][:, k * D:(k + 1) * D], slot[2][:, 0:D]).then_inc(zero_st, 16)
                pool.wait_ge(zero_st, 16 * 8)
            own = [1 if layers > 1 else 0]

            def step(ins):
                own[0] += 1
                ins.then_inc(pool_own, 1)
                pool.wait_ge(pool_own, own[0])

            TT = nc.gpsimd.tensor_tensor
            TS = nc.gpsimd.tensor_scalar

            def cmul(yr, yi, ar, ai, br, bi, t1, t2):
                step(TT(t1, ar, br, ALU.mult))
                step(TT(t2, ai, bi, ALU.mult))
                step(TT(yr, t1, t2, ALU.subtract))
                step(TT(t1, ar, bi, ALU.mult))
                step(TT(t2, ai, br, ALU.mult))
                step(TT(yi, t1, t2, ALU.add))

            def s5_parameters():
                G = GROUPS

                def r(i, n=1):
                    return slot[0][:, i * G:(i + n) * G]
                pool.wait_ge(later_landed, 16 * len(LATER))
                pool.wait_ge(prm_act, 1)
                sn, cs, mag, den = r(6), r(7), r(8), r(2)
                ar, ai = prm[:, 0, :], prm[:, 1, :]
                pr, pi = lam[:, 0, :, :], lam[:, 1, :, :]
                step(TT(pr[:, 0, :], mag, cs, ALU.mult))
                step(TT(pi[:, 0, :], mag, sn, ALU.mult))
                ta = slot[0][:, 12 * G:16 * G].rearrange("p (d g) -> p d g", d=4)
                tb = slot[0][:, 16 * G:20 * G].rearrange("p (d g) -> p d g", d=4)
                for k in (1, 2, 4):
                    bc = lambda v: v[:, k - 1:k, :].to_broadcast([P, k, G])
                    cmul(pr[:, k:2 * k, :], pi[:, k:2 * k, :], pr[:, 0:k, :], pi[:, 0:k, :], bc(pr), bc(pi), ta[:, 0:k, :], tb[:, 0:k, :])
                zr, zi = r(0), r(1)
                step(TS(r(5), pr[:, 0, :], -1.0, None, ALU.add))
                step(TT(r(3), r(5), ar, ALU.mult))
                step(TT(r(4), pi[:, 0, :], ai, ALU.mult))
                step(TT(r(3), r(3), r(4), ALU.add))
                step(TT(zr, r(3), den, ALU.mult))
                step(TT(r(3), pi[:, 0, :], ar, ALU.mult))
                step(TT(r(4), r(5), ai, ALU.mult))
                step(TT(r(3), r(3), r(4), ALU.subtract))
                step(TT(r(3), r(3), den, ALU.mult))
                step(TS(zi, r(3), sgn, None, ALU.mult))
                wide = lambda v: v.unsqueeze(2).to_broadcast([P, G, GC])
                wA = slot[4][:, 0:D].rearrange("p (g c) -> p g c", g=G)
                wB = slot[4][:, D:2 * D].rearrange("p (g c) -> p g c", g=G)
                pool.wait_ge(gate_ps, 1)
                pool.wait_ge(xT_ready, 4)
                step(TT(wA, BB, wide(zi), ALU.mult))
                step(TT(wB, BA, wide(zi), ALU.mult))
                step(TT(BA, BA, wide(zr), ALU.mult))
                step(TT(BA, BA, wA, ALU.add))
                step(TT(BB, BB, wide(zr), ALU.mult))
                step(TT(BB, BB, wB, ALU.subtract))
                step(TS(slot[1][:, D:2 * D], slot[1][:, D:2 * D], sgn, None, ALU.mult))
                step(TS(slot[3][:, 0:D], slot[3][:, 0:D], nsgn, None, ALU.mult))
                step(TS(slot[3][:, D:2 * D], slot[3][:, D:2 * D], -1.0, None, ALU.mult))
                cmul(r(10), r(11), cs, sn, cs, sn, r(3), r(4))
                cmul(r(0), r(1), r(10), r(11), r(10), r(11), r(3), r(4))
                cmul(prm[:, 0, :], prm[:, 1, :], r(0), r(1), r(0), r(1), r(3), r(4))
                step(TT(r(3), mag, mag, ALU.mult))
                step(TT(r(4), r(3), r(3), ALU.mult))
                step(TT(mag8[:, :], r(4), r(4), ALU.mult))
                nc.gpsimd.memset(slot[4][:, 0:1], 0.0).then_inc(lam_ready, 1)

            def s5_tables():
                prg, pig = (lam[:, i, :, :].rearrange("p d g -> p g d") for i in range(2))
                prb, pib = (lam[:, i, 6::-1, :].rearrange("p d g -> p g d") for i in range(2))
                nb = 16
                tC = slot[4][:, 0:nb * P].rearrange("p (g d c) -> p g d c", g=nb, d=STEP)
                tW = slot[4][:, 0:nb * 7 * GC].rearrange("p (g d c) -> p g d c", g=nb, d=7)
                BTs = BT[:, :, :].rearrange("p g (s c) -> p g s c", s=STEP)
                pool.wait_ge(xT_ready, 8)
                for i in range(GROUPS // nb):
                    gs = slice(i * nb, (i + 1) * nb)
                    pw = lambda v, k: v[:, gs, :].unsqueeze(3).to_broadcast([P, nb, k, GC])
                    cw = lambda v, k: v[:, gs, :].unsqueeze(2).to_broadcast([P, nb, k, GC])
                    step(TT(CT[:, gs, :, :], pw(prg, STEP), cw(CA, STEP), ALU.mult))
                    step(TT(tC, pw(pig, STEP), cw(CB, STEP), ALU.mult))
                    step(TT(CT[:, gs, :, :], CT[:, gs, :, :], tC, ALU.add))
                    step(TT(BTs[:, gs, 0:7, :], pw(prb, 7), cw(BA, 7), ALU.mult))
                    step(TT(tW, pw(pib, 7), cw(BB, 7), ALU.mult))
                    step(TT(BTs[:, gs, 0:7, :], BTs[:, gs, 0:7, :], tW, ALU.add))
                    nc.gpsimd.tensor_copy(BTs[:, gs, 7, :], BA[:, gs, :])
                def r(i):
                    return slot[4][:, D // 2 + i * GROUPS:D // 2 + (i + 1) * GROUPS]
                a, sq = (prm[:, 0, :], prm[:, 1, :]), (prm[:, 2, :], turn[:, :])
                nc.gpsimd.memset(cosT[:, :, 0:1], 1.0)
                step(nc.gpsimd.memset(sinT[:, :, 0:1], 0.0))
                k = 1
                while k < NBLK:
                    bc = lambda v: v.unsqueeze(2).to_broadcast([P, GROUPS, k])
                    e1 = slot[4][:, 0:GROUPS * k].rearrange("p (g n) -> p g n", g=GROUPS)
                    e2 = slot[4][:, D:D + GROUPS * k].rearrange("p (g n) -> p g n", g=GROUPS)
                    cmul(cosT[:, :, k:2 * k], sinT[:, :, k:2 * k], cosT[:, :, 0:k], sinT[:, :, 0:k], bc(a[0]), bc(a[1]), e1, e2)
                    if 2 * k < NBLK:
                        cmul(sq[0], sq[1], a[0], a[1], a[0], a[1], r(0), r(1))
                        a, sq = sq, a
                    k *= 2
                step(TS(sinT[:, :, :], sinT[:, :, :], sgn, None, ALU.mult))
                nc.gpsimd.memset(slot[4][:, 0:1], 0.0).then_inc(tables, 1)

            n = 0
            for l in range(layers):
                kind = MIXERS[l]
                if kind == "fox":
                    if l > 0:
                        pool.wait_ge(x_ready, TM * 2 * l)
                    nc.gpsimd.tensor_copy(
                        qa[HD:KQ, :, :], cst[HD:KQ, C_HOT:C_HOT + HEADS].unsqueeze(2).to_broadcast([HEADS, HEADS, SEQ])
                    ).then_inc(qa_rows, 1)
                    if l == 0 and layers > 1:
                        pool.wait_ge(qa_rows, 1)
                        s5_parameters()
                for k in range(2):
                    if kind == "s5" and k == 0:
                        pool.wait_ge(y_ps, 4)
                    if n > 0:
                        pool.wait_ge(x_ready, TM * n)
                    for q in range(2):
                        pool.dma_start(gb[:, q, :], t["ln_row"][q, n].partition_broadcast(P)).then_inc(gb_landed, 16)
                    if n == 1 and layers > 1:
                        s5_tables()
                    pool.wait_ge(gb_landed, 32 * (n + 1))
                    if n == n_ln - 1:
                        break
                    for m in range(TM):
                        pool.wait_ge(xn_ready[m], n + 1)
                        step(TT(x_tm[:, m, :], res[:, m, :], gb[:, 0, :], ALU.mult))
                        TT(x_tm[:, m, :], x_tm[:, m, :], gb[:, 1, :], ALU.add).then_inc(x_ready, 1)
                    n += 1

        @block.scalar
        def _(act):
            nxt = [0]
            own = [0]

            def step(ins):
                own[0] += 1
                ins.then_inc(act_own, 1)
                act.wait_ge(act_own, own[0])

            def hi(c, k=0):
                act.wait_ge(raw_landed[c % RAW], 16 * (c // RAW + 1) + 16 * k)
                if c >= SPL:
                    act.wait_ge(w_used, c - SPL + 1 + RAW * k)
                nc.scalar.activation(whi[:, c % SPL, :], raw[:, c % RAW, :], ACT.Copy).then_inc(w_hi, 1)

            def hi_to(c):
                while nxt[0] <= min(c, n_tiles - 1):
                    hi(nxt[0])
                    nxt[0] += 1

            def ln(n, ahead):
                if n >= 0:
                    nc.scalar.preload_act_table(ACT.Sqrt)
                    for m in range(TM):
                        act.wait_ge(var_ready, TM * n + m + 1)
                        nc.scalar.activation(std[:, m, :], mv[:, m, 1:2], ACT.Sqrt, bias=cst[:, C_EPS:C_EPS + 1]).then_inc(std_ready, 1)
                        if m == 0 and n < n_ln - 1:
                            act.wait_ge(rstd_ready, n + 1)
                            nc.scalar.activation(res[:, 0, :], res[:, 0, :], ACT.Identity, scale=rstd[:, 0, :], bias=nmr[:, :]).then_inc(xn_ready[0], 1)
                    if n == n_ln - 1:
                        return
                hi_to(ahead)
                for b in range(4):
                    if b % 2:
                        act.wait_ge(xnT_ready, 4 * (n + 1) + b + 1)
                        for q in range(2):
                            cols = slice(q * SEQ, (q + 1) * SEQ)
                            k = 2 * b + q
                            if n < 0:
                                ins = nc.scalar.copy(xval[:, b, cols], bank[4 + b][:, cols])
                            else:
                                ins = nc.scalar.activation(xval[:, b, cols], bank[4 + b][:, cols], ACT.Identity,
                                                           scale=ln_col[:, 0, n, k:k + 1], bias=ln_col[:, 1, n, k:k + 1])
                        ins.then_inc(xval_ready[1], 1)
                    act.wait_ge(xval_ready[b % 2], 2 * (n + 1) + b // 2 + 1)
                    nc.scalar.activation(xhi[:, 2 * b:2 * b + 2, :], xval[:, b, :].rearrange("p (k t) -> p k t", k=2), ACT.Copy).then_inc(xhi_ready, 1)

            def ffn(l):
                T0 = starts[l] + MIX_TILES[MIXERS[l]]
                E0 = FCH * l

                def chunk(c, k=0, dc=0):
                    t0 = T0 + 3 * c
                    hi(t0 + 2, k)
                    act.wait_ge(w_used, t0 + (0 if c else 1) + RAW * k)
                    nc.scalar.activation(silu[:, :], bank[4][:, 0:SEQ], ACT.Silu).then_inc(silu_ready, 1)
                    hi(t0 + 3, k)
                    act.wait_ge(h_ready, E0 + c + 1 + 2 * k)
                    nc.scalar.activation(hhi[:, c % 2, :], hval[:, :], ACT.Copy).then_inc(hhi_ready, 1)
                    hi(t0 + 4, k)

                hi_to(T0 + 1)
                nc.scalar.preload_act_table(ACT.Silu)
                with act.Fori(0, (FCH - 2) // 2) as k:
                    chunk(0, k)
                    chunk(1, k)
                chunk(FCH - 2)
                c = FCH - 1
                act.wait_ge(w_used, T0 + 3 * c)
                nc.scalar.activation(silu[:, :], bank[4][:, 0:SEQ], ACT.Silu).then_inc(silu_ready, 1)
                act.wait_ge(h_ready, E0 + c + 1)
                nc.scalar.activation(hhi[:, c % 2, :], hval[:, :], ACT.Copy).then_inc(hhi_ready, 1)
                nxt[0] = T0 + T_FFN - 1
                hi_to(T0 + T_FFN)

            def fox(l, f):
                T0 = starts[l]
                hi_to(T0 + 2)
                act.wait_ge(gate_z, f + 1)
                step(nc.scalar.activation(zg[:, 2, :], zg[:, 1, :], ACT.Exp, scale=-1.0))
                nc.scalar.activation(zg[:, 2, :], zg[:, 2, :], ACT.Ln, bias=1.0).then_inc(gate_l, 1)
                for c in range(KC):
                    hi_to(T0 + c + 2)
                if l == 0 and layers > 1:
                    act.wait_ge(prm_dve, 1)
                    nc.scalar.activation(slot[0][:, 6 * GROUPS:8 * GROUPS], slot[0][:, 4 * GROUPS:6 * GROUPS], ACT.Sin).then_inc(prm_act, 1)
                for j in range(2):
                    act.wait_ge(w_used, T0 + KC)
                    nc.scalar.copy(vt[:, 0, j * HALF:(j + 1) * HALF], bank[j][:, :]).then_inc(v_sb, 1)
                E1 = PAIRS * f
                E2 = HEADS * f
                for j in range(PAIRS + 2):
                    tq = T0 + KC + 2 * j
                    if j < PAIRS:
                        hi_to(tq + 2)
                    if j < PAIRS:
                        act.wait_ge(w_used, tq + 1)
                        for s in range(2):
                            nc.scalar.copy(qa[0:HD, 2 * j + s, :], bank[4][s * HD:(s + 1) * HD, 0:SEQ]).then_inc(q_sb, 1)
                        hi_to(tq + 3)
                    if j >= 2:
                        for s in range(2):
                            act.wait_ge(pT_ps, E2 + 2 * (j - 2) + s + 1)
                            if j >= 3:
                                act.wait_ge(o_ps, E1 + j - 2)
                            nc.scalar.copy(pT[:, s, :], bank[s][:, 0:3 * P]).then_inc(pT_sb, 1)
                    if 1 <= j <= PAIRS:
                        for s in range(2):
                            act.wait_ge(s_sb, E2 + 2 * (j - 1) + s + 1)
                            nc.scalar.activation(sc[:, s, 0:P], sc[:, s, 0:P], ACT.Exp, scale=0.125,
                                                 bias=smx[:, s, 2:3], accum_out=smx[:, s, 4:5])
                            nc.scalar.activation(sc[:, s, P:3 * P], sc[:, s, P:3 * P], ACT.Exp, scale=0.125,
                                                 bias=smx[:, s, 3:4], accum_out=smx[:, s, 5:6]).then_inc(e_sb, 1)
                    if j >= 2:
                        act.wait_ge(o_ps, E1 + j - 1)
                        nc.scalar.copy(ohi[:, j - 2, :], bank[2 + j % 2][:, 0:SEQ]).then_inc(ohi_sb, 1)
                for c in range(KC - 1):
                    hi_to(T0 + KC + 2 * PAIRS + c + 2)

            def s5(l):
                T0 = starts[l]
                for c in range(KC):
                    hi_to(T0 + c + 2)
                    act.wait_ge(wb_ps, 2 * c + 1)
                    nc.scalar.copy(BT[:, 8 * c:8 * c + 4, :], bank[4 + (2 * c) % 4][:, :].rearrange("p (g n) -> p g n", g=4)).then_inc(bt_sb, 1)
                act.wait_ge(x_ready, TM * 2 * l)
                act.wait_ge(w_used, T0 + KC)
                for j in range(2):
                    nc.scalar.copy(u_tm[:, 0, j * HALF:(j + 1) * HALF], bank[j][:, :]).then_inc(u_sb, 1)
                act.wait_ge(u_sb, 4)
                for j in range(4):
                    for m in range(TM):
                        act.dma_start(U2[32 * j + 16 * m:32 * j + 16 * m + 16, :, :], u_tm[:, m, 256 * j:256 * j + 256]).then_inc(u2_ld, 16)
                for b in range(2):
                    act.wait_ge(m_ps, 2 * b + 1)
                    nc.scalar.copy(Msb[:, 8 * b:8 * b + 4, :], bank[4 + 2 * b][:, :].rearrange("p (g n) -> p g n", g=4)).then_inc(m_sb, 1)
                    if b == 0:
                        act.wait_ge(u2_ld, 16 * 8)
                        nc.scalar.copy(Ug[:, 0:8, :, :], U2s[:, 0:8, :, :]).then_inc(ug_sb, 1)
                act.wait_ge(m_d, 1)
                act.wait_ge(zero_st, 16 * 8)
                toep = t["toep"].rearrange("p (g n) -> p g n", g=GROUPS)
                for s in range(STEP):
                    for j in range(4):
                        act.dma_start(toep[s * GC:(s + 1) * GC, 16 * j:16 * j + 16, s * GC:P],
                                      Msb[32 * j:32 * j + GC, :, 0:P - s * GC]).then_inc(m_st, 16)
                act.wait_ge(m_st, 16 * 32)
                for j in range(4):
                    act.wait_ge(uT_ps, j + 1)
                    nc.scalar.copy(Ust[:, 16 * j:16 * j + 16, :], bank[4 + j][:, :].rearrange("p (g n) -> p g n", g=16)).then_inc(uT_sb, 1)
                for j in range(4):
                    act.wait_ge(st_ps, j + 1)
                    act.dma_start(BT[:, 16 * j:16 * j + 16, :], t["toep"][:, j * 2 * D:(j + 1) * 2 * D].rearrange("p (g n) -> p g n", g=16)).then_inc(tp_ld[j], 16)
                    nc.scalar.copy(Ssb[:, 16 * j:16 * j + 16, :], bank[j][:, :].rearrange("p (g n) -> p g n", g=16)).then_inc(st_sb, 1)
                ys = slot[3][:, :].rearrange("p (s g c) -> p g s c", s=STEP, g=16)
                for b in range(4):
                    act.wait_ge(y_ps, b + 1)
                    nc.scalar.activation(ys[:, 4 * b:4 * b + 4, :, :], bank[b][:, :].rearrange("p (g s c) -> p g s c", g=4, s=STEP), ACT.Gelu_apprx_tanh).then_inc(y_sb, 1)
                act.dma_start(bglu, t["b_glu"]).then_inc(bglu_landed, 16)
                act.wait_ge(y_sb, 4)
                for j in range(4):
                    for m in range(TM):
                        act.dma_start(y_tm[:, m, 256 * j:256 * j + 256], slot[3][32 * j + 16 * m:32 * j + 16 * m + 16, :]).then_inc(yt_ld, 16)
                for b in range(4):
                    act.wait_ge(yT_ps, b + 1)
                    nc.scalar.copy(ohi[:, 2 * b:2 * b + 2, :], bank[4 + b][:, :].rearrange("p (k t) -> p k t", k=2)).then_inc(yhi_sb, 1)
                for j in range(2):
                    for c in range(KC):
                        hi_to(min(T0 + KC + j * KC + c + 2, T0 + T_S5))
                    for m in range(TM):
                        if m == 0:
                            act.wait_ge(glu_ps, j + 1)
                        else:
                            act.wait_ge(w_used, T0 + KC + (j + 1) * KC)
                        nc.scalar.activation(slot[1][:, (2 * j + m) * HALF:(2 * j + m + 1) * HALF], bank[4 - 4 * j + 2 * m + 1][:, :], ACT.Sigmoid).then_inc(sig_sb, 1)

            def poolmix(l):
                T0 = starts[l]
                act.wait_ge(later_landed, 16 * len(LATER))
                act.wait_ge(pads_zero, 1)
                for c in range(KC):
                    hi_to(T0 + c + 2)
                    act.wait_ge(w_used, T0 + c + 1)
                    if c >= 2:
                        act.wait_ge(pm_sb, c - 1)
                    nc.scalar.copy(ub[c % 2][:, PADT:], bank[c % 2][:, 0:SEQ]).then_inc(pu_sb, 1)
                    if c >= 1:
                        act.wait_ge(pm_sb, c)
                        nc.scalar.copy(ohi[:, c - 1, :], slot[3][:, ((c - 1) % 2) * SEQ:((c - 1) % 2 + 1) * SEQ]).then_inc(phi_sb, 1)
                act.wait_ge(pm_sb, KC)
                nc.scalar.copy(ohi[:, KC - 1, :], slot[3][:, ((KC - 1) % 2) * SEQ:((KC - 1) % 2 + 1) * SEQ]).then_inc(phi_sb, 1)
                for c in range(2):
                    hi_to(T0 + KC + c + 2)
                    for e in range(4):
                        q = 4 * c + e
                        if e < 3:
                            act.wait_ge(pg_ps, 3 * c + e + 1)
                        else:
                            act.wait_ge(w_used, T0 + KC + c + 1)
                        nc.scalar.activation(xhi[:, q, :], bank[4 + q % 4][:, 0:SEQ], ACT.Copy, scale=pscale[:, q:q + 1]).then_inc(zhi_sb, 1)
                for c in range(KC - 1):
                    hi_to(T0 + KC + 2 + c + 2)

            act.wait_ge(small_landed, 16 * len(FIRST))
            ln(-1, 2)
            n = 0
            f = 0
            for l in range(layers):
                kind = MIXERS[l]
                if kind == "fox":
                    fox(l, f)
                    f += 1
                elif kind == "s5":
                    s5(l)
                else:
                    poolmix(l)
                end = starts[l] + MIX_TILES[kind]
                ln(n, end + 1)
                ffn(l)
                ln(n + 1, end + T_FFN + 2)
                n += 2
            for m in range(TM):
                act.wait_ge(x_ready, TM * (n_ln - 1) + m + 1)
                act.dma_start(t["out"][m * P:(m + 1) * P, :], x_tm[:, m, :]).then_inc(stored, 16)
            act.wait_ge(stored, 16 * TM)

        @block.vector
        def _(dve):
            nxt = [0]
            own = [0]
            V = nc.vector

            def step(ins):
                own[0] += 1
                ins.then_inc(dve_own, 1)
                dve.wait_ge(dve_own, own[0])

            def lo(c, k=0):
                dve.wait_ge(w_hi, c + 1 + RAW * k)
                V.tensor_tensor(wlo[:, c % SPL, :], raw[:, c % RAW, :], whi[:, c % SPL, :].bitcast(F32), ALU.subtract).then_inc(w_lo, 1)

            def lo_to(c):
                while nxt[0] <= min(c, n_tiles - 1):
                    lo(nxt[0])
                    nxt[0] += 1

            def residual(n, m, j, src):
                if n > 0 and j == 0:
                    dve.wait_ge(x_ready, TM * (n - 1) + m + 1)
                cols = slice(j * HALF, (j + 1) * HALF)
                step(V.scalar_tensor_tensor(res[:, m, cols], x_tm[:, m, cols], ALPHA, src, ALU.mult, ALU.add))
                return V.bn_stats(stats[:, m, j, :], res[:, m, cols])

            def mean_rstd(n, m):
                dve.wait_ge(std_ready, TM * n + m + 1)
                step(V.reciprocal(rstd[:, m, :], std[:, m, :]))

            def ln(n, ahead, last_tile=None, glu=None):
                if n >= 0:
                    if n == 0 and layers > 1:
                        dve.wait_ge(lam_ready, 1)
                    for m in range(TM):
                        for j in range(2):
                            if glu is None:
                                b = 2 * m + j
                                if b < 3:
                                    dve.wait_ge(sub_done, 3 * (n - (1 if n > 2 else 0)) + b + 1)
                                else:
                                    dve.wait_ge(w_used, last_tile + 1)
                                ins = residual(n, m, j, bank[b][:, :])
                            elif j == 1:
                                ins = residual(n, m, j, glu(m, j))
                            if m == 1 and j == 0 and n < n_ln - 1:
                                mean_rstd(n, 0)
                                V.tensor_scalar(nmr[:, :], mv[:, 0, 0:1], rstd[:, 0, :], -1.0, ALU.mult, ALU.mult).then_inc(rstd_ready, 1)
                        step(ins)
                        V.bn_aggr(mv[:, m, :], stats[:, m, :, :]).then_inc(var_ready, 1)
                    if n == n_ln - 1:
                        dve.wait_ge(gb_landed, 32 * n_ln)
                        for m in range(TM):
                            dve.wait_ge(var_ready, TM * n + m + 1)
                            step(V.scalar_tensor_tensor(x_tm[:, m, :], res[:, m, :], mv[:, m, 0:1], gb[:, 0, :], ALU.subtract, ALU.mult))
                            mean_rstd(n, m)
                            V.scalar_tensor_tensor(x_tm[:, m, :], x_tm[:, m, :], rstd[:, m, :], gb[:, 1, :], ALU.mult, ALU.add).then_inc(x_ready, 1)
                        return
                    mean_rstd(n, 1)
                    V.tensor_scalar(res[:, 1, :], res[:, 1, :], mv[:, 1, 0:1], rstd[:, 1, :], ALU.subtract, ALU.mult).then_inc(xn_ready[1], 1)
                lo_to(ahead)
                if n == 1 and layers > 1:
                    dve.wait_ge(tables, 1)

                def x_lo(b):
                    dve.wait_ge(xval_ready[b % 2], 2 * (n + 1) + b // 2 + 1)
                    dve.wait_ge(xhi_ready, 4 * (n + 1) + b + 1)
                    V.tensor_tensor(xlo[:, 2 * b:2 * b + 2, :], xval[:, b, :].rearrange("p (k t) -> p k t", k=2),
                                    xhi[:, 2 * b:2 * b + 2, :].bitcast(F32), ALU.subtract).then_inc(xT_ready, 1)
                for b in (0, 2):
                    dve.wait_ge(xnT_ready, 4 * (n + 1) + b + 1)
                    if n < 0:
                        V.tensor_copy(xval[:, b, :], bank[4 + b][:, :]).then_inc(xval_ready[0], 1)
                    else:
                        for q in range(2):
                            cols = slice(q * SEQ, (q + 1) * SEQ)
                            ins = V.tensor_scalar(xval[:, b, cols], bank[4 + b][:, cols], ln_col[:, 0, n, 2 * b + q:2 * b + q + 1],
                                                  ln_col[:, 1, n, 2 * b + q:2 * b + q + 1], ALU.mult, ALU.add)
                        ins.then_inc(xval_ready[0], 1)
                    if b == 0:
                        x_lo(0)
                for b in (1, 2, 3):
                    x_lo(b)

            def ffn(l):
                T0 = starts[l] + MIX_TILES[MIXERS[l]]
                E0 = FCH * l

                def gate(c, k=0):
                    dve.wait_ge(silu_ready, E0 + c + 1 + 2 * k)
                    dve.wait_ge(w_used, T0 + 3 * c + (1 if c else 2) + RAW * k)
                    V.tensor_tensor(hval[:, :], bank[5][:, 0:SEQ], silu[:, :], ALU.mult).then_inc(h_ready, 1)

                def gate_lo(c, k=0):
                    dve.wait_ge(hhi_ready, E0 + c + 1 + 2 * k)
                    V.tensor_tensor(hlo[:, c % 2, :], hval[:, :], hhi[:, c % 2, :].bitcast(F32), ALU.subtract).then_inc(hlo_ready, 1)

                def chunk(c, k=0):
                    t0 = T0 + 3 * c
                    lo(t0 + 2, k)
                    gate(c, k)
                    lo(t0 + 3, k)
                    gate_lo(c, k)
                    lo(t0 + 4, k)
                    dve.wait_ge(hlo_ready, E0 + c + 1 + 2 * k)

                lo_to(T0 + 1)
                with dve.Fori(0, (FCH - 2) // 2) as k:
                    chunk(0, k)
                    chunk(1, k)
                chunk(FCH - 2)
                gate(FCH - 1)
                gate_lo(FCH - 1)
                nxt[0] = T0 + T_FFN - 1
                lo_to(T0 + T_FFN)

            def fox(l, f):
                T0 = starts[l]
                E1, E2 = PAIRS * f, HEADS * f
                lo_to(T0 + 2)
                dve.wait_ge(gate_ps, f + 1)
                step(V.tensor_scalar(zg[:, 0, :], bank[3][0:HEADS, 0:SEQ], bf[:, f:f + 1], None, ALU.add))
                step(V.tensor_scalar(zg[:, 3, :], zg[:, 0, :], -1.0, None, ALU.mult))
                V.tensor_tensor(zg[:, 1, :], zg[:, 0, :], zg[:, 3, :], ALU.max).then_inc(gate_z, 1)
                step(V.tensor_scalar(zg[:, 3, :], zg[:, 3, :], 0.0, 8.0, ALU.max, ALU.mult))
                step(V.memset(ones[:, :], 1.0))
                dve.wait_ge(gate_l, f + 1)
                step(V.scalar_tensor_tensor(zg[:, 1, :], zg[:, 2, :], 8.0, zg[:, 3, :], ALU.mult, ALU.add))
                step(V.tensor_tensor_scan(zg[:, 0, :], ones[:, :], zg[:, 1, :], 0.0, ALU.mult, ALU.add))
                V.tensor_copy(ka[HD:KQ, :, :], zg[:, 0, :].unsqueeze(1).to_broadcast([HEADS, HEADS, SEQ])).then_inc(ka_rows, 1)
                for c in range(KC):
                    lo_to(T0 + c + 2)
                    if l == 0 and layers > 1:
                        s5_angles(c)
                dve.wait_ge(w_used, T0 + KC)
                for j in range(2):
                    V.tensor_copy(vt[:, 1, j * HALF:(j + 1) * HALF], bank[2 + j][:, :]).then_inc(v_sb, 1)
                for j in range(PAIRS + 2):
                    tq = T0 + KC + 2 * j
                    if j < PAIRS:
                        lo_to(tq + 2)
                    if j >= 2:
                        for s in range(2):
                            dve.wait_ge(e_sb, E2 + 2 * (j - 2) + s + 1)
                            step(V.reciprocal(smx[:, s, 6:8], smx[:, s, 4:6]))
                            V.tensor_scalar(sc[:, s, 0:P], sc[:, s, 0:P], smx[:, s, 6:7], None, ALU.mult)
                            V.tensor_scalar(sc[:, s, P:3 * P], sc[:, s, P:3 * P], smx[:, s, 7:8], None, ALU.mult).then_inc(p_sb, 1)
                    if j < PAIRS:
                        dve.wait_ge(w_used, tq + 2)
                        for s in range(2):
                            V.tensor_copy(ka[0:HD, 2 * j + s, :], bank[5][s * HD:(s + 1) * HD, 0:SEQ]).then_inc(k_sb, 1)
                        lo_to(tq + 3)
                    if 1 <= j <= PAIRS:
                        for s in range(2):
                            dve.wait_ge(s_ps, E2 + 2 * (j - 1) + s + 1)
                            if j >= 2:
                                dve.wait_ge(pT_ps, E2 + 2 * (j - 2) + s + 1)
                            V.tensor_tensor_reduce(sc[:, s, 0:P], bank[6 + s][:, 0:P], cst[:, C_MASK + P:C_MASK + 2 * P], 1.0, NEG,
                                                   ALU.add, ALU.max, smx[:, s, 0:1])
                            step(V.tensor_tensor_reduce(sc[:, s, P:3 * P], bank[6 + s][:, P:3 * P], cst[:, C_MASK:C_MASK + 2 * P], 1.0, NEG,
                                                        ALU.add, ALU.max, smx[:, s, 1:2]))
                            V.tensor_scalar(smx[:, s, 2:4], smx[:, s, 0:2], -0.125, None, ALU.mult).then_inc(s_sb, 1)
                    if j >= 2:
                        dve.wait_ge(ohi_sb, E1 + j - 1)
                        V.tensor_tensor(olo[:, j - 2, :], bank[2 + j % 2][:, 0:SEQ], ohi[:, j - 2, :].bitcast(F32), ALU.subtract).then_inc(olo_sb, 1)
                for c in range(KC - 1):
                    lo_to(T0 + KC + 2 * PAIRS + c + 2)

            def vexp(y, x, a, b, ci):
                step(V.tensor_scalar(a, x, 1.4426950408889634, MAGIC, ALU.mult, ALU.add))
                step(V.tensor_scalar(a, a, MAGIC, None, ALU.subtract))
                step(V.tensor_scalar(a, a, -127.0, 128.0, ALU.max, ALU.min))
                step(V.scalar_tensor_tensor(b, a, -LN2_HI, x, ALU.mult, ALU.add))
                step(V.scalar_tensor_tensor(b, a, -LN2_LO, b, ALU.mult, ALU.add))
                step(V.tensor_scalar(ci.bitcast(I32), a, 127.0, float(1 << 23), ALU.add, ALU.mult))
                step(V.tensor_scalar(y, b, EXP_C[0], None, ALU.mult))
                for cf in EXP_C[1:] + [1.0]:
                    step(V.scalar_tensor_tensor(y, y, cf, b, ALU.add, ALU.mult))
                step(V.tensor_scalar(y, y, 1.0, None, ALU.add))
                step(V.tensor_tensor(y, y, ci, ALU.mult))

            def cmul(yr, yi, ar, ai, br, bi, t1, t2):
                step(V.tensor_tensor(t1, ar, br, ALU.mult))
                step(V.tensor_tensor(t2, ai, bi, ALU.mult))
                step(V.tensor_tensor(yr, t1, t2, ALU.subtract))
                step(V.tensor_tensor(t1, ar, bi, ALU.mult))
                step(V.tensor_tensor(t2, ai, br, ALU.mult))
                step(V.tensor_tensor(yi, t1, t2, ALU.add))

            def s5_angles(part):
                def r(i, n=1):
                    return slot[0][:, i * GROUPS:(i + n) * GROUPS]
                ar, ai, ldt = prm[:, 0, :], prm[:, 1, :], prm[:, 2, :]
                dt, th, den, t1, mag, t2 = r(0), r(1), r(2), r(3), r(8), r(10)
                if part == 0:
                    vexp(dt, ldt, t1, t2, r(9))
                if part == 1:
                    step(V.tensor_tensor(th, ai, dt, ALU.mult))
                    step(V.tensor_tensor(r(11), ar, dt, ALU.mult))
                if part == 2:
                    vexp(mag, r(11), t1, t2, r(9))
                if part == 3:
                    step(V.tensor_scalar(t1, th, 1.0 / (2 * np.pi), MAGIC, ALU.mult, ALU.add))
                    step(V.tensor_scalar(t1, t1, MAGIC, None, ALU.subtract))
                    for cpart in TWO_PI:
                        step(V.scalar_tensor_tensor(th, t1, -cpart, th, ALU.mult, ALU.add))
                    step(V.tensor_scalar(r(4), th, np.pi, -np.pi, ALU.min, ALU.max))
                if part == 4:
                    step(V.tensor_scalar(t1, r(4), np.pi / 2, -2 * np.pi, ALU.is_gt, ALU.mult))
                    step(V.scalar_tensor_tensor(t2, r(4), np.pi / 2, t1, ALU.add, ALU.add))
                    step(V.tensor_scalar(r(5), t2, np.pi, -np.pi, ALU.min, ALU.max))
                if part == 5:
                    step(V.tensor_tensor(t1, ar, ar, ALU.mult))
                    step(V.tensor_tensor(t2, ai, ai, ALU.mult))
                    step(V.tensor_tensor(t1, t1, t2, ALU.add))
                    V.reciprocal(den, t1).then_inc(prm_dve, 1)

            def s5(l, n):
                T0 = starts[l]
                G = GROUPS
                for c in range(KC):
                    lo_to(T0 + c + 2)
                    dve.wait_ge(wb_ps, 2 * c + 2)
                    V.tensor_copy(BT[:, 8 * c + 4:8 * c + 8, :], bank[5 + (2 * c) % 4][:, :].rearrange("p (g n) -> p g n", g=4)).then_inc(bt_sb2, 1)
                dve.wait_ge(x_ready, TM * 2 * l)
                dve.wait_ge(w_used, T0 + KC)
                for j in range(2):
                    V.tensor_copy(u_tm[:, 1, j * HALF:(j + 1) * HALF], bank[2 + j][:, :]).then_inc(u_sb, 1)
                tD = hval[:, :].rearrange("p (g c) -> p g c", g=16)
                step(V.tensor_tensor(tD, dcol[:, :].unsqueeze(2).to_broadcast([P, 16, GC]),
                                     cst[:, C_ID16:C_ID16 + GC].unsqueeze(1).to_broadcast([P, 16, GC]), ALU.mult))
                dve.wait_ge(m_ps, 2)
                V.tensor_copy(Msb[:, 4:8, :], bank[5][:, :].rearrange("p (g n) -> p g n", g=4))
                dve.wait_ge(u2_ld, 16 * 8)
                V.tensor_copy(Ug[:, 8:16, :, :], U2s[:, 8:16, :, :]).then_inc(ug_sb, 1)
                dve.wait_ge(m_ps, 4)
                step(V.tensor_copy(Msb[:, 12:16, :], bank[7][:, :].rearrange("p (g n) -> p g n", g=4)))
                dve.wait_ge(m_sb, 2)
                V.tensor_tensor(Msb[:, :, 0:GC], Msb[:, :, 0:GC], tD, ALU.add).then_inc(m_d, 1)
                dec = g3(1)
                step(V.tensor_copy(dec, mag8[:, :].unsqueeze(2).to_broadcast([P, G, NBLK])))
                step(V.memset(dec[:, :, 0:1], 0.0))
                tmp0 = g3(0)
                for j in range(4):
                    q = slice(16 * j, 16 * j + 16)
                    dve.wait_ge(st_sb, j + 1)
                    step(V.tensor_tensor(rot[:, q, :], Ssb[:, q, :], cosT[:, q, :], ALU.mult))
                    dve.wait_ge(sw_ps, j + 1)
                    step(V.tensor_tensor(tmp0[:, q, :], bank[4 + j][:, :].rearrange("p (g n) -> p g n", g=16), sinT[:, q, :], ALU.mult))
                    step(V.tensor_tensor(rot[:, q, :], rot[:, q, :], tmp0[:, q, :], ALU.subtract))
                for j in range(4):
                    c = slice(HALF * j, HALF * (j + 1))
                    V.tensor_tensor_scan(slot[3][:, c], slot[1][:, c], slot[4][:, c], 0.0, ALU.mult, ALU.add).then_inc(g_sb, 1)
                Hs = g3(1)
                dve.wait_ge(g_sb, 4)
                step(V.memset(Hs[:, :, 0:1], 0.0))
                for j in range(4):
                    q = slice(16 * j, 16 * j + 16)
                    step(V.tensor_tensor(rot[:, q, :], Ssb[:, q, :], cosT[:, q, :], ALU.mult))
                    dve.wait_ge(gw_ps, j + 1)
                    step(V.tensor_tensor(tmp0[:, q, :], bank[4 + j][:, :].rearrange("p (g n) -> p g n", g=16), sinT[:, q, :], ALU.mult))
                    V.tensor_tensor(Hs[:, q, 1:NBLK], rot[:, q, 0:NBLK - 1], tmp0[:, q, 0:NBLK - 1], ALU.add).then_inc(hs_sb, 1)
                dve.wait_ge(y_ps, 4)
                V.memset(ones_row, 1.0).then_inc(ones_set, 1)
                for b in range(4):
                    dve.wait_ge(yhi_sb, b + 1)
                    V.tensor_tensor(olo[:, 2 * b:2 * b + 2, :], bank[4 + b][:, :].rearrange("p (k t) -> p k t", k=2),
                                    ohi[:, 2 * b:2 * b + 2, :].bitcast(F32), ALU.subtract).then_inc(ylo_sb, 1)
                def glu(m, j):
                    dve.wait_ge(sig_sb, 2 * j + m + 1)
                    q = slice((2 * j + m) * HALF, (2 * j + m + 1) * HALF)
                    step(V.tensor_tensor(slot[3][:, q], bank[4 - 4 * j + 2 * m][:, :], slot[1][:, q], ALU.mult))
                    return slot[3][:, q]
                for j in range(2):
                    for c in range(KC):
                        lo_to(min(T0 + KC + j * KC + c + 2, T0 + T_S5))
                    for m in range(TM):
                        if j == 0:
                            residual(n, m, 0, glu(m, 0))
                return glu

            def poolmix(l):
                T0 = starts[l]
                V.memset(slot[1][:, 0:6 * 272], 0.0).then_inc(pads_zero, 1)
                dve.wait_ge(pads_zero, 1)
                for c in range(KC):
                    lo_to(T0 + c + 2)
                    w = c // 2
                    u = ub[c % 2]
                    dve.wait_ge(pu_sb, c + 1)
                    s = u
                    off = 0
                    for i in range(w + 1):
                        sh = 1 << i
                        off += sh
                        d = ub[2 + i]
                        step(V.tensor_tensor(d[:, off:], s[:, off:], s[:, off - sh:272 - sh], ALU.add))
                        s = d
                    if c >= 2:
                        dve.wait_ge(plo_sb, c - 1)
                    pm = slot[3][:, (c % 2) * SEQ:(c % 2 + 1) * SEQ]
                    step(V.scalar_tensor_tensor(pm, s[:, PADT:], 1.0 / WINDOWS[w], u[:, PADT:], ALU.mult, ALU.subtract))
                    r = WINDOWS[w] - 1
                    step(V.tensor_tensor(pm[:, 0:r], s[:, PADT:PADT + r], cst[:, C_INV + 16 * w:C_INV + 16 * w + r], ALU.mult))
                    V.tensor_tensor(pm[:, 0:r], pm[:, 0:r], u[:, PADT:PADT + r], ALU.subtract).then_inc(pm_sb, 1)
                    if c >= 1:
                        dve.wait_ge(phi_sb, c)
                        V.tensor_tensor(olo[:, c - 1, :], slot[3][:, ((c - 1) % 2) * SEQ:((c - 1) % 2 + 1) * SEQ], ohi[:, c - 1, :].bitcast(F32), ALU.subtract).then_inc(plo_sb, 1)
                c = KC
                dve.wait_ge(phi_sb, c)
                V.tensor_tensor(olo[:, c - 1, :], slot[3][:, ((c - 1) % 2) * SEQ:((c - 1) % 2 + 1) * SEQ], ohi[:, c - 1, :].bitcast(F32), ALU.subtract).then_inc(plo_sb, 1)
                for c in range(2):
                    lo_to(T0 + KC + c + 2)
                    for e in range(4):
                        q = 4 * c + e
                        dve.wait_ge(zhi_sb, q + 1)
                        V.scalar_tensor_tensor(xlo[:, q, :], bank[4 + q % 4][:, 0:SEQ], pscale[:, q:q + 1], xhi[:, q, :].bitcast(F32), ALU.mult, ALU.subtract).then_inc(zlo_sb, 1)
                for c in range(KC - 1):
                    lo_to(T0 + KC + 2 + c + 2)

            dve.wait_ge(small_landed, 16 * len(FIRST))
            ln(-1, 2)
            n = 0
            f = 0
            for l in range(layers):
                kind = MIXERS[l]
                glu = None
                if kind == "fox":
                    fox(l, f)
                    f += 1
                elif kind == "s5":
                    glu = s5(l, n)
                else:
                    poolmix(l)
                end = starts[l] + MIX_TILES[kind]
                ln(n, end + 1, end - 1, glu)
                ffn(l)
                ln(n + 1, end + T_FFN + 2, end + T_FFN - 1)
                n += 2

        @block.tensor
        def _(pe):
            mm = nc.tensor.matmul

            def x_split(n, kc):
                if n is not None and kc % 2 == 0:
                    pe.wait_ge(xT_ready, 4 * n + kc // 2 + 1)

            def fm(c, k, dst, bhi, blo, chunks=None, w_at=None, n=None):
                chunks = list(range(KC)) if chunks is None else chunks
                w_at = (lambda i: slice(i * P, (i + 1) * P)) if w_at is None else w_at
                s = c % SPL
                for i, kc in enumerate(chunks):
                    x_split(n, kc)
                    wh, wl = whi[:, s, w_at(i)], wlo[:, s, w_at(i)]
                    mm(dst, wh, bhi[:, kc, :], start=(i == 0), stop=False)
                    mm(dst, wh, blo[:, kc, :], start=False, stop=False)
                    ins = mm(dst, wl, bhi[:, kc, :], start=False, stop=(i == len(chunks) - 1))
                return ins

            def tm(c, a_hi, a_lo, banks, first, last, done=None):
                s = c % SPL
                for m in range(TM):
                    cols = slice(m * P, (m + 1) * P)
                    for j in range(2):
                        mm(banks[2 * m + j][:, :], a_hi[:, cols], whi[:, s, j * HALF:(j + 1) * HALF], start=first, stop=False)
                    for j in range(2):
                        mm(banks[2 * m + j][:, :], a_hi[:, cols], wlo[:, s, j * HALF:(j + 1) * HALF], start=False, stop=False)
                    for j in range(2):
                        ins = mm(banks[2 * m + j][:, :], a_lo[:, cols], whi[:, s, j * HALF:(j + 1) * HALF], start=False, stop=last)
                    if done is not None:
                        done(m, ins)
                return ins

            def tm_end(acts, ready):
                ready(0)
                for i, b in ((0, 0), (0, 1), (1, 0), (1, 1), (0, 2), (1, 2), (0, 3), (1, 3)):
                    if (i, b) == (1, 0):
                        ready(1)
                    c, a_hi, a_lo = acts[i]
                    m, s = b // 2, c % SPL
                    cols, half = slice(m * P, (m + 1) * P), slice(b % 2 * HALF, (b % 2 + 1) * HALF)
                    mm(bank[b][:, :], a_hi[:, cols], whi[:, s, half], start=False, stop=False)
                    mm(bank[b][:, :], a_hi[:, cols], wlo[:, s, half], start=False, stop=False)
                    ins = mm(bank[b][:, :], a_lo[:, cols], whi[:, s, half], start=False, stop=(i == 1))
                    if b == 3:
                        used(ins)
                    elif i == 1:
                        ins.then_inc(sub_done, 1)

            def used(ins):
                ins.then_inc(w_used, 1)

            def lnT(n, src):
                for m in range(TM):
                    if n >= 0:
                        pe.wait_ge(xn_ready[m], n + 1)
                    for b in range(4):
                        for q in range(2):
                            ins = nc.tensor.transpose(bank[4 + b][:, q * SEQ + m * P:q * SEQ + (m + 1) * P],
                                                      src[:, m, (2 * b + q) * P:(2 * b + q + 1) * P], ident)
                        if m == TM - 1:
                            ins.then_inc(xnT_ready, 1)

            def ffn(l, n):
                T0 = starts[l] + MIX_TILES[MIXERS[l]]
                E0 = FCH * l
                acc = bank[0:4]

                def up(c, k=0, first=False):
                    t0 = T0 + (3 * c - 1 if not first else 0)
                    pe.wait_ge(w_lo, t0 + 1 + RAW * k)
                    if E0 + c >= 1:
                        pe.wait_ge(silu_ready, E0 + c + 2 * k)
                    ins = fm(t0, k, bank[4][:, 0:SEQ], xhi, xlo, n=n if first else None)
                    used(ins)
                    pe.wait_ge(w_lo, t0 + 2 + RAW * k)
                    if E0 + c >= 1:
                        pe.wait_ge(h_ready, E0 + c + 2 * k)
                    ins = fm(t0 + 1, k, bank[5][:, 0:SEQ], xhi, xlo)
                    used(ins)

                def down(c, k=0, first=False):
                    t = T0 + 3 * c + 4
                    pe.wait_ge(w_lo, t + 1 + RAW * k)
                    pe.wait_ge(hlo_ready, E0 + c + 1 + 2 * k)
                    ins = tm(t, hhi[:, c % 2, :], hlo[:, c % 2, :], acc, first, False)
                    used(ins)

                up(0, first=True)
                up(1)
                down(0, first=True)
                up(2)
                down(1)
                with pe.Fori(0, (FCH - 4) // 2) as k:
                    up(3, k)
                    down(2, k)
                    up(4, k)
                    down(3, k)
                up(FCH - 1)
                t, h = T0 + T_FFN - 2, FCH - 2

                def ready(i):
                    pe.wait_ge(w_lo, t + i + 1)
                    pe.wait_ge(hlo_ready, E0 + h + i + 1)
                tm_end([(t + i, hhi[:, (h + i) % 2, :], hlo[:, (h + i) % 2, :]) for i in range(2)], ready)

            def fox(l, f, n):
                T0 = starts[l]
                E1, E2 = PAIRS * f, HEADS * f
                for kc in range(KC):
                    b = kc // 2
                    if kc % 2 == 0:
                        pe.wait_ge(xval_ready[b % 2], 2 * n + b // 2 + 1)
                    ins = mm(bank[3][0:HEADS, 0:SEQ], wf[:, f, kc, :], xval[:, kc // 2, (kc % 2) * SEQ:(kc % 2 + 1) * SEQ], start=(kc == 0), stop=(kc == KC - 1))
                ins.then_inc(gate_ps, 1)
                for c in range(KC):
                    pe.wait_ge(w_lo, T0 + c + 1)
                    x_split(n, c)

                    def logits_read(m, ins):
                        if m == 0:
                            pe.wait_ge(gate_z, f + 1)
                    used(tm(T0 + c, xhi[:, c, :], xlo[:, c, :], bank[0:4], c == 0, c == KC - 1, logits_read if c == 0 else None))
                for j in range(PAIRS + 2):
                    tq = T0 + KC + 2 * j
                    if j < PAIRS:
                        pe.wait_ge(w_lo, tq + 1)
                        if j >= 1:
                            pe.wait_ge(q_sb, 2 * (E1 + j))
                        ins = fm(tq, 0, bank[4][:, 0:SEQ], xhi, xlo)
                        used(ins)
                        pe.wait_ge(w_lo, tq + 2)
                        if j >= 1:
                            pe.wait_ge(k_sb, 2 * (E1 + j))
                        ins = fm(tq + 1, 0, bank[5][:, 0:SEQ], xhi, xlo)
                        used(ins)
                    if j >= 2:
                        for s in range(2):
                            pe.wait_ge(p_sb, E2 + 2 * (j - 2) + s + 1)
                            if j == 2:
                                pe.wait_ge(v_sb, 4 * (f + 1))
                            else:
                                pe.wait_ge(pT_sb, E2 + 2 * (j - 3) + s + 1)
                            for b in range(3):
                                ins = nc.tensor.transpose(bank[s][:, b * P:(b + 1) * P], sc[:, s, b * P:(b + 1) * P], ident)
                            ins.then_inc(pT_ps, 1)
                    if 1 <= j <= PAIRS:
                        if j == 1:
                            pe.wait_ge(ka_rows, f + 1)
                            pe.wait_ge(qa_rows, f + 1)
                        pe.wait_ge(q_sb, 2 * (E1 + j))
                        pe.wait_ge(k_sb, 2 * (E1 + j))
                        for s in range(2):
                            h = 2 * (j - 1) + s
                            if j >= 2:
                                pe.wait_ge(s_sb, E2 + 2 * (j - 2) + s + 1)
                            mm(bank[6 + s][:, 0:P], qa[:, h, 0:P], ka[:, h, 0:P], start=True, stop=True)
                            mm(bank[6 + s][:, P:3 * P], qa[:, h, P:SEQ], ka[:, h, :], start=True, stop=True).then_inc(s_ps, 1)
                    if j >= 2:
                        o = bank[2 + j % 2]
                        if j >= 4:
                            pe.wait_ge(olo_sb, E1 + j - 3)
                        for s in range(2):
                            h = 2 * (j - 2) + s
                            pe.wait_ge(pT_sb, E2 + h + 1)
                            dst = slice(s * HD, (s + 1) * HD)
                            mm(o[dst, 0:SEQ], vt[:, 0, h * HD:(h + 1) * HD], pT[:, s, 0:SEQ], start=True, stop=False)
                            ins = mm(o[dst, P:SEQ], vt[:, 1, h * HD:(h + 1) * HD], pT[:, s, SEQ:3 * P], start=False, stop=True)
                        ins.then_inc(o_ps, 1)
                T1 = T0 + KC + 2 * PAIRS
                pe.wait_ge(olo_sb, E1 + PAIRS)
                for c in range(KC - 2):
                    pe.wait_ge(w_lo, T1 + c + 1)
                    used(tm(T1 + c, ohi[:, c, :], olo[:, c, :], bank[0:4], c == 0, False))
                tm_end([(T1 + c, ohi[:, c, :], olo[:, c, :]) for c in (KC - 2, KC - 1)],
                       lambda i: pe.wait_ge(w_lo, T1 + KC - 2 + i + 1))

            def s5(l, n):
                T0 = starts[l]
                pe.wait_ge(tables, 1)
                for c in range(KC):
                    pe.wait_ge(w_lo, T0 + c + 1)
                    x_split(n, c)
                    used(tm(T0 + c, xhi[:, c, :], xlo[:, c, :], bank[0:4], c == 0, c == KC - 1))
                    for i in range(2):
                        if c >= 2:
                            pe.wait_ge((bt_sb, bt_sb2)[i], c - 1)
                        else:
                            pe.wait_ge(xval_ready[i], 2 * n + c + 1)
                        for g in range(4):
                            ins = nc.tensor.transpose(bank[4 + (2 * c + i) % 4][:, g * P:(g + 1) * P], BT[:, 8 * c + 4 * i + g, :], ident)
                        ins.then_inc(wb_ps, 1)
                pe.wait_ge(bt_sb, KC)
                pe.wait_ge(bt_sb2, KC)
                for b in range(4):
                    for q in range(4):
                        for j in range(4):
                            g = 16 * j + 4 * b + q
                            lhs = slot[1][:, g * GC:g * GC + 32]
                            mm(bank[4 + b][32 * j:32 * j + 32, q * P:q * P + GC], lhs, CA[:, g, :], start=True, stop=True)
                            ins = mm(bank[4 + b][32 * j:32 * j + 32, q * P + GC:(q + 1) * P], lhs,
                                     CT[:, g, 0:STEP - 1, :].rearrange("p d c -> p (d c)"), start=True, stop=True)
                    ins.then_inc(m_ps, 1)
                pe.wait_ge(ug_sb, 2)
                pe.wait_ge(m_d, 1)
                for j in range(4):
                    for g in range(16):
                        ins = nc.tensor.transpose(bank[4 + j][:, g * NBLK:(g + 1) * NBLK], slot[0][32 * j:32 * j + 32, g * P:(g + 1) * P],
                                                  cst[32 * j:32 * j + 32, C_ID + 32 * j:C_ID + 32 * j + 32])
                    ins.then_inc(uT_ps, 1)
                for j in range(4):
                    pe.wait_ge(uT_sb, j + 1)
                    for g in range(16):
                        ins = mm(bank[j][:, g * NBLK:(g + 1) * NBLK], BT[:, 16 * j + g, :], Ust[:, 16 * j + g, :], start=True, stop=True)
                    ins.then_inc(st_ps, 1)
                perm = cst[:, C_PERM:C_PERM + P]
                for j in range(4):
                    pe.wait_ge(st_sb, j + 1)
                    mm(bank[4 + j][:, :], perm, slot[3][:, j * HALF:(j + 1) * HALF], start=True, stop=True).then_inc(sw_ps, 1)
                pe.wait_ge(st_sb, 4)

                def y_at(g):
                    j, b, q = g // 16, g % 16 // 4, g % 4
                    return bank[b][32 * j:32 * j + 32, q * P:(q + 1) * P], (0, 32 * j)
                for g in range(GROUPS):
                    if g % 16 == 0:
                        pe.wait_ge(tp_ld[g // 16], 16)
                    dst, pos = y_at(g)
                    mm(dst, Ust[:, g, :], BT[:, g, :], start=(g % 4 == 0), stop=False, tile_position=pos, skip_group_check=True)
                for j in range(4):
                    pe.wait_ge(g_sb, 4)
                    mm(bank[4 + j][:, :], perm, slot[3][:, j * HALF:(j + 1) * HALF], start=True, stop=True).then_inc(gw_ps, 1)
                pe.wait_ge(hs_sb, 4)
                for b in range(4):
                    for q in range(4):
                        for j in range(4):
                            g = 16 * j + 4 * b + q
                            dst, pos = y_at(g)
                            ins = mm(dst, slot[1][:, g * NBLK:(g + 1) * NBLK], CT[:, g, :, :].rearrange("p d c -> p (d c)"),
                                     start=False, stop=True, tile_position=pos, skip_group_check=True)
                    ins.then_inc(y_ps, 1)
                def bias(j, b):
                    v = b % 2
                    mm(bank[4 - 4 * j + b][:, :], ones_row, bglu[:, v * D + j * HALF:v * D + (j + 1) * HALF], start=True, stop=False)
                pe.wait_ge(ones_set, 1)
                pe.wait_ge(bglu_landed, 16)
                for b in range(4):
                    pe.wait_ge(y_sb, b + 1)
                    bias(1, b)
                pe.wait_ge(yt_ld, 16 * 8)
                for b in range(4):
                    for q in range(2):
                        for m in range(TM):
                            ins = nc.tensor.transpose(bank[4 + b][:, q * SEQ + m * P:q * SEQ + (m + 1) * P], y_tm[:, m, (2 * b + q) * P:(2 * b + q + 1) * P], ident)
                    ins.then_inc(yT_ps, 1)
                T1 = T0 + KC
                for b in range(4):
                    pe.wait_ge(ylo_sb, b + 1)
                    bias(0, b)
                for j in range(2):
                    banks = bank[4 - 4 * j:8 - 4 * j]
                    for c in range(KC):
                        pe.wait_ge(w_lo, T1 + j * KC + c + 1)

                        def done(m, ins):
                            if m == 0:
                                ins.then_inc(glu_ps, 1)
                        ins = tm(T1 + j * KC + c, ohi[:, c, :], olo[:, c, :], banks, False, c == KC - 1, done if c == KC - 1 else None)
                        used(ins)

            def poolmix(l, n):
                T0 = starts[l]
                for c in range(KC):
                    pe.wait_ge(w_lo, T0 + c + 1)
                    if c >= 2:
                        pe.wait_ge(pu_sb, c - 1)
                    ins = fm(T0 + c, 0, bank[c % 2][:, 0:SEQ], xhi, xlo, n=n if c == 0 else None)
                    used(ins)
                T1 = T0 + KC
                for c in range(2):
                    pe.wait_ge(w_lo, T1 + c + 1)
                    for gl in range(2):
                        gi = 2 * c + gl
                        pe.wait_ge(plo_sb, 2 * gi + 2)
                        for e in range(2):
                            q = 2 * gi + e
                            if q >= 4:
                                pe.wait_ge(zlo_sb, q - 3)
                            ins = fm(T1 + c, 0, bank[4 + q % 4][:, 0:SEQ], ohi, olo, chunks=[2 * gi, 2 * gi + 1],
                                     w_at=lambda i: slice((gl * 4 + i * 2 + e) * P, (gl * 4 + i * 2 + e + 1) * P))
                            if gl == 1 and e == 1:
                                used(ins)
                            else:
                                ins.then_inc(pg_ps, 1)
                T2 = T1 + 2
                pe.wait_ge(zlo_sb, KC)
                for c in range(KC - 2):
                    pe.wait_ge(w_lo, T2 + c + 1)
                    used(tm(T2 + c, xhi[:, c, :], xlo[:, c, :], bank[0:4], c == 0, False))
                tm_end([(T2 + c, xhi[:, c, :], xlo[:, c, :]) for c in (KC - 2, KC - 1)],
                       lambda i: pe.wait_ge(w_lo, T2 + KC - 2 + i + 1))

            pe.wait_ge(small_landed, 16 * len(FIRST))
            pe.wait_ge(x_landed, 16)
            lnT(-1, x_tm)
            n = 0
            f = 0
            for l in range(layers):
                kind = MIXERS[l]
                if kind == "fox":
                    fox(l, f, n)
                    f += 1
                elif kind == "s5":
                    s5(l, n)
                else:
                    poolmix(l, n)
                lnT(n, res)
                ffn(l, n + 1)
                if n + 1 < n_ln - 1:
                    lnT(n + 1, res)
                n += 2


def _pack(w):
    tiles = []

    def fm(a, c):
        tiles.append(a[:, c * P:(c + 1) * P].reshape(KC, P, P).transpose(1, 0, 2).reshape(P, D))

    def tm(a, kc):
        tiles.append(a[kc * P:(kc + 1) * P, :])

    seen = {"fox": 0, "s5": 0, "pool": 0}
    for l, kind in enumerate(MIXERS):
        i = seen[kind]
        seen[kind] += 1
        if kind == "fox":
            qkv = w["fox_w_qkv"][i]
            for kc in range(KC):
                tm(qkv[:, 2 * D:], kc)
            for j in range(PAIRS):
                fm(qkv[:, 0:D], j)
                fm(qkv[:, D:2 * D], j)
            for kc in range(KC):
                tm(w["fox_w_o"][i], kc)
        elif kind == "s5":
            for kc in range(KC):
                tm(w["s5_w_in"][i], kc)
            for j in range(2):
                for kc in range(KC):
                    rows = w["s5_w_glu"][i][kc * P:(kc + 1) * P]
                    tiles.append(np.concatenate([rows[:, j * HALF:(j + 1) * HALF], rows[:, D + j * HALF:D + (j + 1) * HALF]], 1))
        else:
            for c in range(KC):
                fm(w["pool_w_in"][i], c)
            for c in range(2):
                g = w["pool_w_grp"][i][2 * c:2 * c + 2].reshape(2, 2, P, 2, P)
                tiles.append(g.transpose(2, 0, 1, 3, 4).reshape(P, D))
            for kc in range(KC):
                tm(w["pool_w_out"][i], kc)
        w1, w3, w2 = w["ffn_w1"][l], w["ffn_w3"][l], w["ffn_w2"][l]
        for c in range(FCH + 1):
            if c < FCH:
                fm(w1, c)
                fm(w3, c)
            if c >= 1:
                tm(w2, c - 1)
    return np.stack(tiles)


def kernel(**inputs):
    import concourse.bacc as bacc
    from concourse.bass_utils import run_bass_kernel_spmd

    w = {k: np.asarray(v) for k, v in inputs.items()}

    def col(a):
        return np.ascontiguousarray(np.moveaxis(a.reshape(*a.shape[:-1], KC, P), -1, 0))

    def state_rows(top, bottom):
        return np.concatenate([top.swapaxes(0, 1), bottom.swapaxes(0, 1)], 0)

    are, aim, ldt = w["s5_a_re"][0], w["s5_a_im"][0], w["s5_log_dt"][0]
    br, bi = w["s5_b_re"][0], w["s5_b_im"][0]
    cr, ci = (w[k][0].transpose(0, 2, 1) for k in ("s5_c_re", "s5_c_im"))
    ldt = np.broadcast_to(ldt[:, None], are.shape)
    dcol = np.zeros((4, 2, GC, 16), np.float32)
    dcol[:, 0] = w["s5_d"][0].reshape(4, 16, GC).transpose(0, 2, 1)
    arrays = {
        "x": w["x"][0],
        "w": _pack(w),
        "consts": constants(),
        "ln_col": col(np.stack([w["ln_g"].reshape(2 * DEPTH, D), w["ln_b"].reshape(2 * DEPTH, D)])),
        "ln_row": np.stack([w["ln_g"].reshape(2 * DEPTH, D), w["ln_b"].reshape(2 * DEPTH, D)]),
        "wf": w["fox_w_f"].reshape(2, KC, P, HEADS).transpose(2, 0, 1, 3),
        "bf": w["fox_b_f"].T,
        "s5_prm": np.stack([state_rows(v, v) for v in (are, aim, ldt)], 1),
        "s5_dcol": dcol.reshape(P, 16),
        "s5_B": np.stack([state_rows(br, bi), state_rows(bi, br)], 1).reshape(P, 2 * D),
        "s5_C": np.stack([state_rows(cr, ci), state_rows(ci, cr)], 1).reshape(P, 2 * D),
        "pool_scale": col(w["pool_scale"][0]),
        "b_glu": w["s5_b_glu"],
    }
    nc = bacc.Bacc("TRN2", target_bir_lowering=False, num_devices=1)
    in_map, t = {}, {}
    for name, a in arrays.items():
        a = np.ascontiguousarray(a)
        in_map[f"in_{name}"] = a
        t[name] = nc.dram_tensor(f"in_{name}", a.shape, mybir.dt.from_np(a.dtype), kind="ExternalInput").ap()
    t["toep"] = nc.dram_tensor("toep", (P, GROUPS * P), F32, kind="Internal").ap()
    t["out"] = nc.dram_tensor("out", (SEQ, D), F32, kind="ExternalOutput").ap()
    build(nc, t)
    r = run_bass_kernel_spmd(nc, [in_map], core_ids=[0])
    return r.results[0]["out"].reshape(1, SEQ, D)
```
